# Optimizing a Trainium2 kernel written in Bass

```python
import jax, jax.numpy as jnp
from jax import lax
import numpy as np

D_MODEL = 1024
BATCH = 1
SEQ = 1024
DEPTH = 1

PLE_DIM = 256
N_HEADS = 16
N_KV_HEADS = 2
HEAD_DIM = 64
GROUP = N_HEADS // N_KV_HEADS
ATTN_WIDTH = N_HEADS * HEAD_DIM
KV_WIDTH = N_KV_HEADS * HEAD_DIM
CONV_WIDTH = D_MODEL
CONV_KERNEL = 31
WINDOW = 128
BLOCK = 128
ROPE_DIM = HEAD_DIM // 4
ROPE_THETA = 500000.0
N_BRANCH = 2
EPS = 1e-6
MAX_POS_OFFSET = 1024

COL_SIZES = (CONV_WIDTH, CONV_WIDTH, CONV_WIDTH,
             ATTN_WIDTH, KV_WIDTH, KV_WIDTH, ATTN_WIDTH,
             D_MODEL, D_MODEL)
IN_WIDTH = sum(COL_SIZES)

kernel_name = "hybrid_conformer_conv_swa_sink_gated_merge"

def rmsnorm(x, g):
    xf = x.astype(jnp.float32)
    y = xf * lax.rsqrt(jnp.mean(xf * xf, axis=-1, keepdims=True) + EPS)
    return (y * g.astype(jnp.float32)).astype(x.dtype)

def layernorm(x, g, b):
    xf = x.astype(jnp.float32)
    mu = jnp.mean(xf, axis=-1, keepdims=True)
    var = jnp.mean(jnp.square(xf - mu), axis=-1, keepdims=True)
    y = (xf - mu) * lax.rsqrt(var + EPS)
    return (y * g.astype(jnp.float32) + b.astype(jnp.float32)).astype(x.dtype)

def split_columns(z):
    outs, start = [], 0
    for size in COL_SIZES:
        outs.append(z[..., start:start + size])
        start += size
    return outs

def conformer_conv(val, glu_gate, w_dw, b_dw, ln_g, ln_b, w_pw):
    u = val * jax.nn.sigmoid(glu_gate)
    c = lax.conv_general_dilated(
        u, w_dw[:, None, :].astype(u.dtype), window_strides=(1,),
        padding=[(CONV_KERNEL - 1, 0)],
        dimension_numbers=('NWC', 'WIO', 'NWC'),
        feature_group_count=CONV_WIDTH) + b_dw
    c = jax.nn.silu(layernorm(c, ln_g, ln_b))
    return c @ w_pw

def rope_tables(positions, dtype):
    inv = jnp.power(ROPE_THETA, -jnp.arange(0, ROPE_DIM, 2, dtype=jnp.float32) / ROPE_DIM)
    ang = positions.astype(jnp.float32)[..., None] * inv
    return jnp.cos(ang)[:, :, None, :].astype(dtype), jnp.sin(ang)[:, :, None, :].astype(dtype)

def partial_rope(t, cos, sin):
    half = ROPE_DIM // 2
    t1 = t[..., :half]
    t2 = t[..., half:ROPE_DIM]
    return jnp.concatenate([t1 * cos - t2 * sin, t2 * cos + t1 * sin, t[..., ROPE_DIM:]], axis=-1)

def sliding_window_sink_attention(q, k, v, sinks, positions):
    B, S = q.shape[0], q.shape[1]
    nb = S // BLOCK
    q = q.reshape(B, S, N_HEADS, HEAD_DIM)
    k = k.reshape(B, S, N_KV_HEADS, HEAD_DIM)
    v = v.reshape(B, S, N_KV_HEADS, HEAD_DIM)
    cos, sin = rope_tables(positions, q.dtype)
    q = partial_rope(q, cos, sin)
    k = partial_rope(k, cos, sin)
    q = q.reshape(B, nb, BLOCK, N_KV_HEADS, GROUP, HEAD_DIM)
    k = k.reshape(B, nb, BLOCK, N_KV_HEADS, HEAD_DIM)
    v = v.reshape(B, nb, BLOCK, N_KV_HEADS, HEAD_DIM)
    pad = ((0, 0), (1, 0), (0, 0), (0, 0), (0, 0))
    kb = jnp.concatenate([jnp.pad(k[:, :-1], pad), k], axis=2)
    vb = jnp.concatenate([jnp.pad(v[:, :-1], pad), v], axis=2)
    s = jnp.einsum('bnqkgd,bnskd->bnkgqs', q, kb).astype(jnp.float32) * (HEAD_DIM ** -0.5)
    qi = jnp.arange(BLOCK)[:, None]
    sj = jnp.arange(2 * BLOCK)[None, :]
    band = (sj <= qi + BLOCK) & (sj > qi + BLOCK - WINDOW)
    blk = jnp.arange(nb)[:, None, None]
    mask = band[None] & ((blk > 0) | (sj[None] >= BLOCK))
    s = jnp.where(mask[None, :, None, None], s, -jnp.inf)
    sink = jnp.broadcast_to(sinks.astype(jnp.float32).reshape(1, 1, N_KV_HEADS, GROUP, 1, 1),
                            s.shape[:-1] + (1,))
    probs = jax.nn.softmax(jnp.concatenate([s, sink], axis=-1), axis=-1)[..., :-1]
    o = jnp.einsum('bnkgqs,bnskd->bnqkgd', probs.astype(vb.dtype), vb)
    return o.reshape(B, S, ATTN_WIDTH)

def setup_inputs(seed: int = 0) -> dict:
    key = jax.random.key(seed)
    ks = jax.random.split(key, 20)
    f32 = jnp.float32
    x = jax.random.normal(ks[0], (BATCH, SEQ, D_MODEL), f32)
    p = jax.random.normal(ks[1], (DEPTH, BATCH, SEQ, PLE_DIM), f32)
    offsets = jax.random.randint(ks[2], (BATCH, 1), 0, MAX_POS_OFFSET, dtype=jnp.int32)
    positions = offsets + jnp.arange(SEQ, dtype=jnp.int32)[None, :]
    w_in = jax.random.normal(ks[3], (DEPTH, D_MODEL, IN_WIDTH), f32) * D_MODEL ** -0.5
    ln_pre = 1.0 + 0.05 * jax.random.normal(ks[4], (DEPTH, D_MODEL), f32)
    ln_post = 1.0 + 0.05 * jax.random.normal(ks[5], (DEPTH, D_MODEL), f32)
    w_dw = jax.random.normal(ks[6], (DEPTH, CONV_KERNEL, CONV_WIDTH), f32) * CONV_KERNEL ** -0.5
    b_dw = 0.02 * jax.random.normal(ks[7], (DEPTH, CONV_WIDTH), f32)
    conv_ln_g = 1.0 + 0.05 * jax.random.normal(ks[8], (DEPTH, CONV_WIDTH), f32)
    conv_ln_b = 0.02 * jax.random.normal(ks[9], (DEPTH, CONV_WIDTH), f32)
    w_pw = jax.random.normal(ks[10], (DEPTH, CONV_WIDTH, CONV_WIDTH), f32) * CONV_WIDTH ** -0.5
    sinks = 0.5 * jax.random.normal(ks[11], (DEPTH, N_HEADS), f32)
    w_br_conv = jax.random.normal(ks[12], (DEPTH, CONV_WIDTH, D_MODEL), f32) * CONV_WIDTH ** -0.5
    w_br_attn = jax.random.normal(ks[13], (DEPTH, ATTN_WIDTH, D_MODEL), f32) * ATTN_WIDTH ** -0.5
    w_out = jax.random.normal(ks[14], (DEPTH, D_MODEL, D_MODEL), f32) * D_MODEL ** -0.5
    w_ple_gate = jax.random.normal(ks[15], (DEPTH, D_MODEL, D_MODEL), f32) * D_MODEL ** -0.5
    w_ple_proj = jax.random.normal(ks[16], (DEPTH, PLE_DIM, D_MODEL), f32) * PLE_DIM ** -0.5
    return {"x": x, "p": p, "positions": positions, "w_in": w_in, "ln_pre": ln_pre,
            "ln_post": ln_post, "w_dw": w_dw, "b_dw": b_dw, "conv_ln_g": conv_ln_g,
            "conv_ln_b": conv_ln_b, "w_pw": w_pw, "sinks": sinks, "w_br_conv": w_br_conv,
            "w_br_attn": w_br_attn, "w_out": w_out, "w_ple_gate": w_ple_gate,
            "w_ple_proj": w_ple_proj}

def reference(x, p, positions, w_in, ln_pre, ln_post, w_dw, b_dw, conv_ln_g, conv_ln_b,
              w_pw, sinks, w_br_conv, w_br_attn, w_out, w_ple_gate, w_ple_proj):
    for i in range(DEPTH):
        h = rmsnorm(x, ln_pre[i])
        z = h @ w_in[i]
        (c_val, c_glu, c_gate, q, k, v, a_gate, g_conv, g_attn) = split_columns(z)
        ya = conformer_conv(c_val, c_glu, w_dw[i], b_dw[i], conv_ln_g[i], conv_ln_b[i], w_pw[i])
        ya = (ya * jax.nn.silu(c_gate)) @ w_br_conv[i]
        yb = sliding_window_sink_attention(q, k, v, sinks[i], positions)
        yb = (yb * jax.nn.silu(a_gate)) @ w_br_attn[i]
        m = jax.nn.sigmoid(g_conv) * ya + jax.nn.sigmoid(g_attn) * yb
        x = x + rmsnorm(m @ w_out[i], ln_post[i])
        x = x + jax.nn.sigmoid(x @ w_ple_gate[i]) * (p[i] @ w_ple_proj[i])
    return x


_drawn_inputs = setup_inputs


def setup_inputs(seed=0):
    import zlib

    import numpy as np

    out = dict(_drawn_inputs(seed))
    spreads = {}
    factors = {'conv_ln_b': 4.323, 'sinks': 8.0}
    for name, (base, spread) in spreads.items():
        noise = np.random.default_rng([zlib.crc32(name.encode()), seed]).standard_normal(out[name].shape)
        drawn = base * np.exp(spread * noise) if base else spread * noise
        out[name] = __import__('jax').numpy.asarray(drawn.astype(out[name].dtype))
    for name, factor in factors.items():
        out[name] = (out[name] * factor).astype(out[name].dtype)
    return out
```

```python
from contextlib import ExitStack

import concourse.bass as bass
from concourse import mybir

F32 = mybir.dt.float32
F32R = mybir.dt.float32r
I32 = mybir.dt.int32
U32 = mybir.dt.uint32
ALU = mybir.AluOpType
ACT = mybir.ActivationFunctionType
AX_X = mybir.AxisListType.X

P = 128
D = 1024
S = 1024
KT = D // P
HALF = 512
PLE_KT = 2
TAPS = 31
PAD = TAPS - 1
HEADS = 16
NB = S // P
HD = 64
EPS = 1e-6
SCALE = HD ** -0.5
NEG = -3.0e38
MAGIC = 12582912.0
TWO_PI = (6.28125, 0.0019350051879882812, 3.0199159819567e-07)

A0 = 0
K_TILE, V_TILE = 32, 33
Q0 = 34
C0 = 42
D0 = 50
E0 = 58
F0 = 66
G0 = 74
H0 = 82
I0 = 98
TILES = 114
WTILES = 98
PLE_STEPS = 2

COL = {name: 8 * j for j, name in enumerate(("ln_pre", "ln_post", "ln_g", "ln_b", "b_dw"))}
COL_TAPS = 40
COL_INV = COL_TAPS + KT * TAPS
COL_SGN = COL_INV + 1
NCOL = COL_SGN + 1


def build(nc, dram):
    with ExitStack() as ctx:
        def sem(name):
            return ctx.enter_context(nc.semaphore(name))

        KB = 1024
        start = (nc.sbuf_base + 31) // 32 * 32
        RA, RB, RC, RD, RE = (start + 32 * KB * j for j in range(5))
        W = start + 160 * KB
        G = W + 24 * KB

        def at(name, shape, dt, offset):
            return nc.alloc_sbuf_tensor_at(name, [P] + shape, dt, offset=offset)

        h_hi = at("h_hi", [KT, S], F32R, RA)
        h_lo = at("h_lo", [KT, S], F32R, RB)
        conv = at("conv", [KT, S], F32, RC)
        qo = at("qo", [KT, S], F32, RD)
        p_raw = at("p_raw", [PLE_KT, S], F32, RD)
        p_hi = at("p_hi", [PLE_KT, S], F32R, RD + 8 * KB)
        p_lo = at("p_lo", [PLE_KT, S], F32R, RD + 16 * KB)
        u_off = RD + 24 * KB
        u = at("u", [PAD + S], F32, u_off)
        kdup = at("kdup", [2, S], F32, RE)
        vkeys = at("vkeys", [NB, P], F32, RE + 8 * KB)
        cos_t = at("cos_t", [S], F32, RE + 12 * KB)
        sin_t = at("sin_t", [S], F32, RE + 16 * KB)
        rtmp = at("rtmp", [S], F32, RE + 20 * KB)
        v_t = at("v_t", [S], F32, RE + 24 * KB)
        k_raw = at("k_raw", [S], F32, RE + 28 * KB)
        probs = at("probs", [HEADS, P], F32, RE + 12 * KB)
        pt_cur = at("pt_cur", [2, HALF], F32, RE + 20 * KB)
        pt_prev = at("pt_prev", [2, HALF], F32, RE + 24 * KB)
        kblk = at("kblk", [2, 2 * P], F32, RE + 28 * KB)
        vblk = at("vblk", [2, P], F32, RE + 30 * KB)
        o_hi = at("o_hi", [KT, S], F32R, RE)
        o_lo = at("o_lo", [KT, S], F32R, RD)
        merged = at("merged", [KT, S], F32, RA)
        c_hi = at("c_hi", [KT, S], F32R, RB)
        c_lo = at("c_lo", [KT, S], F32R, RC)
        y_hi = at("y_hi", [KT, S], F32R, RE)
        y_lo = at("y_lo", [KT, S], F32R, RD)
        m_hi = at("m_hi", [KT, S], F32R, RB)
        m_lo = at("m_lo", [KT, S], F32R, RA)
        wout = at("wout", [KT, S], F32, RC)
        x1_hi = at("x1_hi", [KT, S], F32R, RE)
        x1_lo = at("x1_lo", [KT, S], F32R, RD)
        result = at("result", [KT, S], F32, RA)

        w_raw = at("w_raw", [2, KT * P], F32, W)
        w_hi = at("w_hi", [2, KT * P], F32R, W + 8 * KB)
        w_lo = at("w_lo", [2, KT * P], F32R, W + 16 * KB)

        tanh_t = at("tanh_t", [S], F32, G)
        diag = at("diag", [NB, P], F32, G)
        tanh_h = at("tanh_h", [HALF], F32, G + 2 * KB)
        ring_h = at("ring_h", [2, 2, HALF], F32, G + 4 * KB)
        ring = at("ring", [2, S], F32, G + 4 * KB)
        work = at("work", [S], F32, G + 12 * KB)
        square = at("square", [HALF], F32, G + 14 * KB)
        q_blk = at("q_blk", [KT, P], F32, G + 12 * KB)
        sums = at("sums", [S], F32, G + 16 * KB)
        ident = at("ident", [P], F32, G + 20 * KB)
        ones = at("ones", [P], F32, G + 20 * KB + 512)
        upper = at("upper", [P], F32, G + 21 * KB)
        upper_q = at("upper_q", [P], F32, G + 21 * KB + 512)
        cols = at("cols", [NCOL], F32, G + 22 * KB)
        small = G + 22 * KB + 4 * ((NCOL + 7) // 8 * 8)
        names = {}
        for name, n in (("half_g", KT), ("half_b", KT), ("mean_sq", 8), ("rstd", 8), ("expo", 8), ("sinks", 16),
                        ("smax", 16), ("nmax", 16), ("esink", 16), ("denom", 16), ("rden", 16)):
            names[name] = at(name, [n], F32, small)
            small += 4 * n
        half_g, half_b, mean_sq, rstd, expo = (names[n] for n in ("half_g", "half_b", "mean_sq", "rstd", "expo"))
        sinks, smax, nmax, esink, denom, rden = (names[n] for n in ("sinks", "smax", "nmax", "esink", "denom", "rden"))
        assert small <= nc.sbuf_usable_end

        psg = ctx.enter_context(nc.psum_tensor("psg", [P, 2, S], F32))
        psb = ctx.enter_context(nc.psum_tensor("psb", [P, 4, HALF], F32))

        consts_loaded = sem("consts_loaded")
        pos_loaded = sem("pos_loaded")
        p_loaded = [sem("p_loaded0"), sem("p_loaded1")]
        x_loaded = [sem(f"x_loaded{k}") for k in range(KT)]
        w_loaded = [sem("w_loaded0"), sem("w_loaded1")]
        w_hi_ready = sem("w_hi_ready")
        w_lo_ready = sem("w_lo_ready")
        tile_done = sem("tile_done")
        ps_free = [sem("ps_free0"), sem("ps_free1")]
        spilled = [sem("spilled0"), sem("spilled1")]
        gate_loaded = [sem("gate_loaded0"), sem("gate_loaded1")]
        tanh_ready = sem("tanh_ready")
        tanh_used = sem("tanh_used")
        vec = sem("vec")
        act_own = sem("act_own")
        pool_own = sem("pool_own")
        sq_made = sem("sq_made")
        trig_ready = sem("trig_ready")
        init_done = sem("init_done")
        p_hi_ready = sem("p_hi_ready")
        p_lo_ready = sem("p_lo_ready")
        ang_ready = sem("ang_ready")
        sin_ready = sem("sin_ready")
        sq_ready = sem("sq_ready")
        sq_used = sem("sq_used")
        var_summed = sem("var_summed")
        msq_done = sem("msq_done")
        msq_ready = sem("msq_ready")
        rstd_ready = sem("rstd_ready")
        diag_ready = sem("diag_ready")
        bcast_done = sem("bcast_done")
        full_ready = sem("full_ready")
        hi_ready = sem("hi_ready")
        lo_ready = sem("lo_ready")
        conv_done = sem("conv_done")
        csum_done = sem("csum_done")
        x_again = [sem("x_again0"), sem("x_again1")]
        ple_loaded = [sem("ple_loaded0"), sem("ple_loaded1")]
        rb_ready = sem("rb_ready")
        qk_ready = sem("qk_ready")
        vb_ready = sem("vb_ready")
        mean_done = sem("mean_done")
        centred = sem("centred")
        qk_raw = sem("qk_raw")
        rope_done = sem("rope_done")
        k_dup = sem("k_dup")
        v_turned = sem("v_turned")
        v_ready = sem("v_ready")
        q_ready = sem("q_ready")
        scores_done = sem("scores_done")
        cur_copied = sem("cur_copied")
        prev_used = sem("prev_used")
        max_ready = sem("max_ready")
        exp_done = sem("exp_done")
        exp_own = sem("exp_own")
        probs_ready = sem("probs_ready")
        turned = sem("turned")
        pt_ready = sem("pt_ready")
        pv_done = sem("pv_done")
        o_ready = sem("o_ready")
        ln_scaled = sem("ln_scaled")
        ln_tanh = sem("ln_tanh")
        ln_full = sem("ln_full")
        out_ready = sem("out_ready")
        stored = sem("stored")

        XT, PT, WALL, COLS, CONST, POS, SINKS, OUT = (dram[n] for n in (
            "xT", "pT", "weights", "cols", "masks", "positions", "sinks_b", "outT"))
        GATES, PLE = dram["gates"], dram["ple"]

        banks01 = psb[:, 0:2, :].rearrange("p b s -> p (b s)")

        def score_banks(gp):
            return psb[:, 2 * (gp % 2):2 * (gp % 2) + 2, :].rearrange("p b (h k) -> p (b h) k", h=2)

        def col(name, k):
            return cols[:, k + COL[name]:k + COL[name] + 1]

        class Chain:
            def __init__(self, eng, s):
                self.eng, self.s, self.base, self.n = eng, s, 0, 0

            def step(self, ins):
                ins.then_inc(self.s, 1)
                self.n += 1

            def wait(self):
                self.eng.wait_ge(self.s, self.base + self.n)

            def enter(self, i, per, first=0):
                self.before, self.per = self.base + self.n, per
                self.base, self.n = (i - first) * per + self.before, 0

            def leave(self, times):
                assert self.n == self.per, (self.n, self.per)
                self.base, self.n = self.before + self.per * times, 0

        block = ctx.enter_context(nc.Block())

        @block.sync
        def _(sp):
            def load_weights(step, slot, need=None):
                if need is not None:
                    sp.wait_ge(w_lo_ready, need)
                sp.dma_start(w_raw[:, slot, :], WALL[:, step, :]).then_inc(w_loaded[slot], 16)

            load_weights(0, 0)
            for k in range(PLE_KT):
                sp.dma_start(p_raw[:, k, :], PT[:, k, :]).then_inc(p_loaded[k], 16)
            for k in range(3):
                sp.dma_start(conv[:, k, :], XT[:, k, :]).then_inc(x_loaded[k], 16)
            load_weights(1, 1)
            for k in range(3, KT):
                sp.dma_start(conv[:, k, :], XT[:, k, :]).then_inc(x_loaded[k], 16)
            sp.dma_start(cols[:], COLS).then_inc(consts_loaded, 16)
            sp.dma_start(ident[:], CONST[:, 0, :]).then_inc(consts_loaded, 16)
            sp.dma_start(upper[:], CONST[:, 1, :]).then_inc(consts_loaded, 16)
            sp.dma_start(upper_q[:], CONST[:, 2, :]).then_inc(consts_loaded, 16)
            sp.dma_start(sinks[:], SINKS).then_inc(consts_loaded, 16)
            sp.dma_start(k_raw[:].bitcast(I32), POS).then_inc(pos_loaded, 16)
            with sp.Fori(0, H0 // 2) as i:
                for j in range(2):
                    load_weights(i * 2 + (PLE_STEPS + j), j, i * 2 + (j + 1))
            for first, tiles in ((H0, H0), (H0 + KT, H0), (I0, H0 + KT), (I0 + KT, H0 + KT)):
                with sp.Fori(0, KT // 2) as i:
                    for j in range(2):
                        load_weights(i * 2 + (tiles + PLE_STEPS + j), j, i * 2 + (first + j + 1))
            for h in range(2):
                with sp.Fori(0, KT) as m:
                    sp.wait_ge(out_ready, m + (KT * h + 2))
                    sp.dma_start(OUT[:, m, h * HALF:(h + 1) * HALF],
                                 result[:, m, h * HALF:(h + 1) * HALF]).then_inc(stored, 16)
            sp.wait_ge(stored, 16 * 2 * KT)

        @block.tensor
        def _(pe):
            def product(slot, rhs_hi, rhs_lo, ready=None, kts=KT, wslot=0, wk=0, halves=(0, 1), between=None):
                for k in range(kts):
                    if between is not None and k == kts - 1:
                        between()
                    if ready is not None:
                        pe.wait_ge(lo_ready, ready + k + 1)
                    passes = ((w_hi, rhs_hi), (w_lo, rhs_hi), (w_hi, rhs_lo))
                    for n, (w, r) in enumerate(passes):
                        for h in halves:
                            mm = nc.tensor.matmul(psg[:, slot, h * HALF:(h + 1) * HALF],
                                                  w[:, wslot, (wk + k) * P:(wk + k + 1) * P],
                                                  r[:, k, h * HALF:(h + 1) * HALF],
                                                  start=(k == 0 and n == 0), stop=(k == kts - 1 and n == 2))
                mm.then_inc(tile_done, 1)

            def tile(a2, j, rhs_hi, rhs_lo, ready=None, halves=(0, 1), between=None):
                pe.wait_ge(w_lo_ready, a2 * 2 + (j + PLE_STEPS + 1))
                pe.wait_ge(ps_free[j], a2 + 4)
                product(j, rhs_hi, rhs_lo, ready, wslot=j, halves=halves, between=between)

            def pairs(first, last, rhs_hi, rhs_lo, ready=None, halves=(0, 1)):
                with pe.Fori(first // 2, last // 2) as i:
                    tile(i, 0, rhs_hi, rhs_lo, ready, halves)
                    tile(i, 1, rhs_hi, rhs_lo, None, halves)

            def pair(first, rhs_hi, rhs_lo, ready, halves):
                tile(first // 2, 0, rhs_hi, rhs_lo, ready, halves)
                tile(first // 2, 1, rhs_hi, rhs_lo, None, halves)

            def mean_square(ready, count, blocks=range(NB)):
                pe.wait_ge(ready, count)
                for c in blocks:
                    mm = nc.tensor.matmul(psb[:, 2, c:c + 1], sums[:, c * P:(c + 1) * P], ones[:, 0:1],
                                          start=True, stop=True)
                mm.then_inc(msq_done, 1)

            def broadcast(n, banks=(0, 1)):
                pe.wait_ge(diag_ready, n)
                dg = diag[:].rearrange("p c q -> p (c q)")
                for h, bank in enumerate(banks):
                    mm = nc.tensor.matmul(psb[:, bank, :], ones[:], dg[:, h * HALF:(h + 1) * HALF], start=True, stop=True)
                mm.then_inc(bcast_done, 1)

            pe.wait_ge(init_done, 1)
            pe.wait_ge(p_lo_ready, PLE_KT)
            for t in range(KT):
                if t % 4 == 0:
                    pe.wait_ge(w_lo_ready, t // 4 + 1)
                if t >= 2:
                    pe.wait_ge(ps_free[t % 2], t // 2)
                product(t % 2, p_hi, p_lo, kts=PLE_KT, wslot=t // 4, wk=(t % 4) * PLE_KT)
            mean_square(sq_used, KT)
            broadcast(1)
            pairs(A0, Q0 + 2, h_hi, h_lo, 0)
            pe.wait_ge(csum_done, KT)
            for h in range(2):
                mm = nc.tensor.matmul(psb[:, h, :], ones[:], sums[:, h * HALF:(h + 1) * HALF], start=True, stop=True)
            mm.then_inc(mean_done, 1)
            pairs(Q0 + 2, C0, h_hi, h_lo)
            pe.wait_ge(ps_free[1], 4 + V_TILE // 2 + 1)
            for c in range(NB):
                mm = nc.tensor.transpose(psb[:, 2 + c // 4, (c % 4) * P:(c % 4 + 1) * P], v_t[:, c * P:(c + 1) * P], ident[:])
            mm.then_inc(v_turned, 1)
            pe.wait_ge(centred, KT)

            def attention(n, first, slot, c2):
                pe.wait_ge(qk_ready, n * 2 + 2)
                for gp in range(4):
                    g, par = gp // 2, gp % 2
                    if gp == 0 and not first:
                        pe.wait_ge(pt_ready, n * 4)
                    if gp == 1 and not first:
                        pe.wait_ge(o_ready, n * 2)
                    if gp >= 2:
                        pe.wait_ge(prev_used, n * 4 + (gp - 1))
                    rows = slice(par * HD, par * HD + HD)
                    for j in range(4):
                        c = j % 2 * 2 * P
                        rhs = kblk[rows, g, P:] if first else kblk[rows, g, :]
                        mm = nc.tensor.matmul(psb[:, 2 * par + j // 2, c + (P if first else 0):c + 2 * P],
                                              q_blk[rows, 4 * g + j, :], rhs, start=True, stop=True)
                    mm.then_inc(scores_done, 1)

                def transposes(gp):
                    pe.wait_ge(probs_ready, n * 2 + (gp // 2 + 1))
                    if gp >= 2:
                        pe.wait_ge(pt_ready, n * 4 + (gp - 1))
                    for j in range(4):
                        mm = nc.tensor.transpose(psb[:, gp % 2, j * P:(j + 1) * P], probs[:, 4 * gp + j, :], ident[:])
                    mm.then_inc(turned, 1)

                tile(c2, slot, h_hi, h_lo, between=lambda: transposes(0))
                transposes(1)
                for gp in range(4):
                    g, par = gp // 2, gp % 2
                    if gp in (1, 2):
                        transposes(gp + 1)
                    if gp == 0:
                        pe.wait_ge(vb_ready, n + 1)
                    pe.wait_ge(pt_ready, n * 4 + (gp + 1))
                    out = psb[par * HD:(par + 1) * HD, 2 + g, :]
                    mm = nc.tensor.matmul(out, vblk[:, 1, g * HD:(g + 1) * HD], pt_cur[:, gp % 2, :], start=True, stop=first)
                    if not first:
                        mm = nc.tensor.matmul(out, vblk[:, 0, g * HD:(g + 1) * HD], pt_prev[:, gp % 2, :], start=False, stop=True)
                    mm.then_inc(pv_done, 1)

            pe.wait_ge(v_ready, 1)
            attention(0, True, 0, C0 // 2)
            pe.wait_ge(o_ready, 2)
            mean_square(var_summed, KT + 1)
            pe.wait_ge(msq_ready, 2)
            attention(1, False, 1, C0 // 2)
            pe.wait_ge(pt_ready, 8)
            broadcast(2)
            pe.wait_ge(rb_ready, 1)
            with pe.Fori(1, NB // 2) as i:
                attention(i * 2, False, 0, i + C0 // 2)
                attention(i * 2 + 1, False, 1, i + C0 // 2)
            pairs(D0, E0, h_hi, h_lo)
            pairs(E0, F0, o_hi, o_lo, KT)
            pairs(F0, G0, c_hi, c_lo, 2 * KT)
            pairs(G0, H0, y_hi, y_lo, 3 * KT)
            pairs(H0, H0 + KT, m_hi, m_lo, 4 * KT, (0,))
            H1, I1 = H0 + KT, I0 + KT
            pair(H1, m_hi, m_lo, None, (1,))
            mean_square(sq_used, 2 * KT, range(NB // 2))
            pair(H1 + 2, m_hi, m_lo, None, (1,))
            broadcast(3, (0,))
            pairs(H1 + 4, I0, m_hi, m_lo, None, (1,))
            pair(I0, x1_hi, x1_lo, 5 * KT, (0,))
            mean_square(sq_used, 3 * KT, range(NB // 2, NB))
            pair(I0 + 2, x1_hi, x1_lo, None, (0,))
            broadcast(4, (1,))
            pairs(I0 + 4, I1, x1_hi, x1_lo, None, (0,))
            pairs(I1, TILES, x1_hi, x1_lo, 6 * KT, (1,))

        @block.gpsimd
        def _(pool):
            own = Chain(pool, pool_own)
            nc.gpsimd.memset(ones[:], 1.0).then_inc(init_done, 1)
            own.step(nc.gpsimd.memset(expo[:], -0.5))

            def low_part(step, slot):
                pool.wait_ge(w_hi_ready, step + 1)
                nc.gpsimd.tensor_tensor(w_lo[:, slot, :], w_raw[:, slot, :], w_hi[:, slot, :].bitcast(F32),
                                        ALU.subtract).then_inc(w_lo_ready, 1)

            def low(a2, j):
                low_part(a2 * 2 + (PLE_STEPS + j), j % 2)

            def rsqrt(n, c=slice(0, NB)):
                pool.wait_ge(msq_ready, n)
                own.wait()
                nc.gpsimd.tensor_tensor(rstd[:, c], mean_sq[:, c], expo[:, c], ALU.pow).then_inc(rstd_ready, 1)

            def add_conv(i):
                pool.wait_ge(conv_done, i + 2)
                pool.wait_ge(csum_done, i)
                nc.gpsimd.tensor_tensor(sums[:], sums[:], conv[:, i, :], ALU.add).then_inc(csum_done, 1)

            low_part(0, 0)
            low_part(1, 1)
            rsqrt(1)
            own.step(nc.gpsimd.memset(sums[:], 0.0))
            own.wait()
            low(0, 0)
            for j in range(1, 5):
                low(0, j)
            with pool.Fori(1, KT) as i:
                low(i * 2, 1)
                low(i * 2, 2)
                add_conv(i - 1)
                low(i * 2, 3)
                low(i * 2, 4)
            low(V_TILE // 2, 1)
            low(Q0 // 2, 0)
            add_conv(KT - 1)
            low(Q0 // 2, 1)
            pool.wait_ge(mean_done, 1)
            nc.gpsimd.memset(sums[:], 0.0).then_inc(var_summed, 1)
            pool.wait_ge(spilled[0], 16 * 12)
            with pool.Fori(0, KT // 2) as i:
                low(i + Q0 // 2 + 1, 0)
                low(i + Q0 // 2 + 1, 1)
                for j in range(2):
                    c = i * 2 + j
                    pool.wait_ge(centred, c + 1)
                    pool.wait_ge(var_summed, c + 1)
                    nc.gpsimd.tensor_tensor(ring[:, 0, :], conv[:, c, :], conv[:, c, :], ALU.mult).then_inc(sq_made, 1)
                    pool.wait_ge(sq_made, c + 1)
                    nc.gpsimd.tensor_tensor(sums[:], sums[:], ring[:, 0, :], ALU.add).then_inc(var_summed, 1)
            rsqrt(2)

            def lows(first, last):
                with pool.Fori(first // 2, last // 2) as i:
                    low(i, 0)
                    low(i, 1)

            lows(Q0 + 10, H0 + KT + 4)
            rsqrt(3, slice(0, NB // 2))
            lows(H0 + KT + 4, I0 + 4)
            rsqrt(4, slice(NB // 2, NB))
            lows(I0 + 4, TILES)

        @block.scalar
        def _(act):
            def settled():
                act.nop(nofuse=True)

            def high(a2, j):
                act.wait_ge(w_loaded[j % 2], (a2 + j // 2) * 16 + 32)
                act.wait_ge(tile_done, a2 * 2 + (j + KT - 1))
                nc.scalar.activation(w_hi[:, j % 2, :], w_raw[:, j % 2, :], ACT.Copy).then_inc(w_hi_ready, 1)

            def product_done(a2, j):
                act.wait_ge(tile_done, a2 * 2 + (j + KT + 1))

            def read_out(a2, j):
                act.wait_ge(ps_free[j], a2 + 5)

            def split_high(dst, k, src, index, scale=1.0):
                settled()
                nc.scalar.activation(dst[:, k, :], src, ACT.Copy, scale=scale).then_inc(hi_ready, 1)

            def spill(dst, slot):
                act.dma_start(dst, ring[:, slot, :]).then_inc(spilled[slot], 16)

            act.wait_ge(w_loaded[0], 16)
            nc.scalar.activation(w_hi[:, 0, :], w_raw[:, 0, :], ACT.Copy).then_inc(w_hi_ready, 1)
            for k in range(PLE_KT):
                act.wait_ge(p_loaded[k], 16)
                nc.scalar.activation(p_hi[:, k, :], p_raw[:, k, :], ACT.Copy).then_inc(p_hi_ready, 1)
            squares = (tanh_t, work)

            def square_x(k):
                act.wait_ge(x_loaded[k], 16)
                if k >= 2:
                    act.wait_ge(sq_used, k - 1)
                nc.scalar.activation(squares[k % 2][:], conv[:, k, :], ACT.Square).then_inc(sq_ready, 1)

            square_x(0)
            square_x(1)
            act.wait_ge(w_loaded[1], 16)
            nc.scalar.activation(w_hi[:, 1, :], w_raw[:, 1, :], ACT.Copy).then_inc(w_hi_ready, 1)
            for t in range(KT):
                act.wait_ge(tile_done, t + 1)
                if t >= 2:
                    act.wait_ge(spilled[t % 2], 16 * (t // 2))
                nc.scalar.activation(ring[:, t % 2, :], psg[:, t % 2, :], ACT.Copy).then_inc(ps_free[t % 2], 1)
                act.wait_ge(ps_free[t % 2], t // 2 + 1)
                spill(PLE[:, t, :], t % 2)
                for k in range(2 * t + 2, min(2 * t + 4, KT)):
                    square_x(k)
            high(0, 0)
            for k in range(KT):
                act.wait_ge(full_ready, k + 1)
                split_high(h_hi, k, conv[:, k, :], k)
            act.wait_ge(ang_ready, 1)
            nc.scalar.activation(sin_t[:], cos_t[:], ACT.Sin)
            nc.scalar.activation(v_t[:], cos_t[:], ACT.Sin, scale=0.5).then_inc(sin_ready, 1)

            with act.Fori(0, KT) as i:
                a2 = i * 2
                high(a2, 1)
                product_done(a2, 0)
                act.wait_ge(ps_free[1], i * 2 + 3)
                nc.scalar.activation(tanh_t[:], psg[:, 0, :], ACT.Tanh, scale=0.5).then_inc(ps_free[0], 1)
                high(a2, 2)
                high(a2, 3)
                product_done(a2, 2)
                act.wait_ge(spilled[0], i * 16 + 64)
                nc.scalar.activation(ring[:, 0, :], psg[:, 0, :], ACT.Tanh, scale=0.5).then_inc(ps_free[0], 1)
                act.wait_ge(ps_free[0], i * 2 + 6)
                spill(GATES[:, i + 2 * KT, :], 0)
                high(a2, 4)
                product_done(a2, 3)
                act.wait_ge(spilled[1], i * 16 + 64)
                nc.scalar.activation(ring[:, 1, :], psg[:, 1, :], ACT.Tanh, scale=0.5).then_inc(ps_free[1], 1)
                act.wait_ge(ps_free[1], i * 2 + 6)
                spill(GATES[:, i, :], 1)
            high(K_TILE // 2, 1)
            product_done(K_TILE // 2, 0)
            nc.scalar.activation(k_raw[:], psg[:, 0, :], ACT.Copy).then_inc(qk_raw, 1)
            high(K_TILE // 2, 2)
            product_done(K_TILE // 2, 1)
            act.wait_ge(trig_ready, 1)
            nc.scalar.activation(v_t[:], psg[:, 1, :], ACT.Copy).then_inc(ps_free[1], 1)
            with act.Fori(0, KT // 2) as i:
                for j in range(2):
                    high(i + Q0 // 2, j + 1)
                    product_done(i + Q0 // 2, j)
                    if j == 0:
                        act.wait_ge(conv_done, KT + 1)
                    settled()
                    nc.scalar.activation(qo[:, i * 2 + j, :], psg[:, j, :], ACT.Copy).then_inc(qk_raw, 1)
            act.wait_ge(rope_done, 1)
            for g in range(2):
                for half in range(2):
                    act.dma_start(kdup[half * HD:(half + 1) * HD, g, :], k_raw[g * HD:(g + 1) * HD, :]).then_inc(k_dup, 16)
            act.wait_ge(v_turned, 1)
            nc.scalar.activation(vkeys[:].rearrange("p c d -> p (c d)"), psb[:, 2:4, :].rearrange("p b s -> p (b s)"),
                                 ACT.Copy).then_inc(v_ready, 1)

            def load_qk(n, first=False):
                settled()
                nc.scalar.activation(q_blk[:], qo[:, :, bass.ds(n * P, P)], ACT.Copy).then_inc(qk_ready, 1)
                if first:
                    nc.scalar.activation(kblk[:, :, P:], kdup[:, :, 0:P], ACT.Copy).then_inc(qk_ready, 1)
                else:
                    settled()
                    nc.scalar.activation(kblk[:], kdup[:, :, bass.ds(n * P - P, 2 * P)], ACT.Copy).then_inc(qk_ready, 1)

            def load_v(n, first=False):
                if first:
                    nc.scalar.activation(vblk[:, 1, :], vkeys[:, 0, :], ACT.Copy).then_inc(vb_ready, 1)
                else:
                    settled()
                    nc.scalar.activation(vblk[:], vkeys[:, bass.ds(n - 1, 2), :], ACT.Copy).then_inc(vb_ready, 1)

            act.wait_ge(rope_done, 1 + KT)
            act.wait_ge(k_dup, 64)
            act.wait_ge(v_ready, 1)
            load_qk(0, True)
            load_v(0, True)

            def attention(n, first, last, c2, slot, third=False):
                high(c2, slot + 1)
                for gp in range(4):
                    act.wait_ge(scores_done, n * 4 + (gp + 1))
                    if gp == 0 and not first:
                        act.wait_ge(turned, n * 4)
                    nc.scalar.activation(probs[:, 4 * gp:4 * gp + 4, :], score_banks(gp)[:, :, P:], ACT.Copy).then_inc(cur_copied, 1)
                for g in range(2):
                    act.wait_ge(max_ready, n * 2 + (g + 1))
                    for h in range(8 * g, 8 * g + 8):
                        nc.scalar.activation(probs[:, h, :], probs[:, h, :], ACT.Exp, bias=nmax[:, h:h + 1], scale=SCALE,
                                             accum_out=denom[:, h:h + 1])
                    nc.scalar.activation(esink[:, 8 * g:8 * g + 8], esink[:, 8 * g:8 * g + 8], ACT.Exp).then_inc(exp_done, 1)
                product_done(c2, slot)
                if not first:
                    act.wait_ge(ps_free[1 - slot], c2 + 4 + slot)
                if third:
                    act.wait_ge(bcast_done, 2)
                nc.scalar.activation(tanh_t[:], psg[:, slot, :], ACT.Tanh, scale=0.5).then_inc(tanh_ready, 1)
                if not last:
                    act.wait_ge(scores_done, n * 4 + 4)
                    load_qk(n + 1)
                for g in range(2):
                    act.wait_ge(pv_done, n * 4 + (2 * g + 2))
                    settled()
                    nc.scalar.activation(qo[:, 4 * g:4 * g + 4, bass.ds(n * P, P)],
                                         psb[:, 2 + g, :].rearrange("p (m q) -> p m q", m=4), ACT.Copy).then_inc(o_ready, 1)
                if not last:
                    load_v(n + 1)
                read_out(c2, slot)
                spill(GATES[:, n + KT, :], slot)

            c2 = C0 // 2
            attention(0, True, False, c2, 0)
            attention(1, False, False, c2, 1)
            with act.Fori(1, NB // 2 - 1) as i:
                attention(i * 2, False, False, i + c2, 0, True)
                attention(i * 2 + 1, False, False, i + c2, 1)
            attention(NB - 2, False, False, c2 + NB // 2 - 1, 0)
            attention(NB - 1, False, True, c2 + NB // 2 - 1, 1)

            act.wait_ge(spilled[0], 16 * 16)
            act.wait_ge(spilled[1], 16 * 16)
            with act.Fori(0, KT // 2) as i:
                a2 = i + D0 // 2
                for j in range(2):
                    m = i * 2 + j
                    high(a2, j + 1)
                    act.wait_ge(ln_scaled, m + 1)
                    act.wait_ge(ln_full, m + 1 if j == 0 else m)
                    settled()
                    nc.scalar.activation(ring[:, j, :], conv[:, m, :], ACT.Tanh, bias=half_b[:, bass.ds(m, 1)],
                                         scale=half_g[:, bass.ds(m, 1)]).then_inc(ln_tanh, 1)
                    product_done(a2, j)
                    act.wait_ge(full_ready, m + KT)
                    nc.scalar.activation(tanh_t[:], psg[:, j, :], ACT.Tanh, scale=0.5).then_inc(tanh_ready, 1)
                    act.wait_ge(full_ready, m + (KT + 1))
                    split_high(o_hi, m, qo[:, m, :], m, 0.5)
            act.wait_ge(ln_full, KT + 1)

            def load_gate(r, slot, a2):
                act.wait_ge(ps_free[slot], a2 + 4)
                act.dma_start(ring[:, slot, :], GATES[:, r, :]).then_inc(gate_loaded[slot], 16)

            with act.Fori(0, KT // 2) as i:
                a2 = i + E0 // 2
                for j in range(2):
                    m = i * 2 + j
                    high(a2, j + 1)
                    load_gate(m, j, a2)
                    if j == 0:
                        act.wait_ge(tile_done, E0 + KT)
                    split_high(c_hi, m, conv[:, m, :], m, 0.5)
            with act.Fori(0, KT // 2) as i:
                a2 = i + F0 // 2
                for j in range(2):
                    m = i * 2 + j
                    high(a2, j + 1)
                    load_gate(m + KT, j, a2)
                    read_out(a2, j)
                    split_high(y_hi, m, work[:], m, 0.5)
            with act.Fori(0, KT // 2) as i:
                a2 = i + G0 // 2
                for j in range(2):
                    m = i * 2 + j
                    high(a2, j + 1)
                    load_gate(m + 2 * KT, j, a2)
                    act.wait_ge(full_ready, m + (2 * KT + 1))
                    split_high(m_hi, m, merged[:, m, :], m, 0.5)
            def x_back(h, k):
                act.dma_start(ring_h[:, 0, k % 2, :], XT[:, k, h * HALF:(h + 1) * HALF]).then_inc(x_again[k % 2], 16)

            def ple_back(h, m, j):
                act.dma_start(ring_h[:, 1, j, :], PLE[:, m, h * HALF:(h + 1) * HALF]).then_inc(ple_loaded[j], 16)

            for k in range(2):
                x_back(0, k)
                ple_back(0, k, k)

            def w_out_tile(a2, j, m, h):
                half = slice(h * HALF, (h + 1) * HALF)
                high(a2, j + 1)
                product_done(a2, j)
                settled()
                nc.scalar.activation(wout[:, m, half], psg[:, j, half], ACT.Copy)
                act.wait_ge(sq_used, m + (h + 1) * KT)
                nc.scalar.activation(square[:], psg[:, j, half], ACT.Square).then_inc(ps_free[j], 1)

            def x1_high(h, k):
                half = slice(h * HALF, (h + 1) * HALF)
                act.wait_ge(full_ready, (3 + h) * KT + k + 1)
                nc.scalar.activation(x1_hi[:, k, half], wout[:, k, half], ACT.Copy).then_inc(hi_ready, 1)
                if (h, k) < (1, KT - 2):
                    x_back(h + (k + 2) // KT, (k + 2) % KT)

            def gate_tile(a2, j, m, h, more=True, again=True):
                half = slice(h * HALF, (h + 1) * HALF)
                if more:
                    high(a2, j + 1)
                product_done(a2, j)
                act.wait_ge(tanh_used, m + (h * KT + 1))
                if again:
                    ple_back(*again)
                nc.scalar.activation(tanh_h[:], psg[:, j, half], ACT.Tanh, scale=0.5).then_inc(ps_free[j], 1)

            with act.Fori(0, KT // 2) as i:
                for j in range(2):
                    w_out_tile(i + H0 // 2, j, i * 2 + j, 0)
            for m in range(KT):
                w_out_tile((H0 + KT + m) // 2, m % 2, m, 1)
                if 3 <= m < 7:
                    x1_high(0, 2 * m - 6)
                    x1_high(0, 2 * m - 5)
            for m in range(KT):
                gate_tile((I0 + m) // 2, m % 2, m, 0, again=(0, m + 1, (m + 1) % 2) if 1 <= m < KT - 1
                          else (1, 0, 0) if m == KT - 1 else None)
                if 3 <= m < 7:
                    x1_high(1, 2 * m - 6)
                    x1_high(1, 2 * m - 5)
            with act.Fori(0, KT // 2 - 1) as i:
                for j in range(2):
                    m = i * 2 + j
                    gate_tile(i + (I0 + KT) // 2, j, m, 1, again=(1, m + 1, (j + 1) % 2))
            gate_tile(TILES // 2 - 1, 0, KT - 2, 1, again=(1, KT - 1, 1))
            gate_tile(TILES // 2 - 1, 1, KT - 1, 1, more=False, again=None)

        @block.vector
        def _(dve):
            own = Chain(dve, vec)
            stt = nc.vector.scalar_tensor_tensor

            def product_done(a2, j):
                dve.wait_ge(tile_done, a2 * 2 + (j + KT + 1))

            def split_low(dst, hi, k, src, count, scale=1.0):
                dve.wait_ge(hi_ready, count)
                stt(dst[:, k, :], src, scale, hi[:, k, :].bitcast(F32), ALU.mult, ALU.subtract).then_inc(lo_ready, 1)

            def variance(n, c=slice(0, NB)):
                dve.wait_ge(msq_done, n)
                nc.vector.tensor_scalar(mean_sq[:, c], psb[:, 2, c], 1.0 / D, EPS, ALU.mult, ALU.add).then_inc(msq_ready, 1)

            def diagonal(n, c=slice(0, NB)):
                k = c.stop - c.start
                dve.wait_ge(rstd_ready, n)
                nc.vector.tensor_tensor(diag[:, 0:k, :], ident[:].rearrange("p (a q) -> p a q", a=1).to_broadcast([P, k, P]),
                                        rstd[:, c].rearrange("p (c a) -> p c a", a=1).to_broadcast([P, k, P]),
                                        ALU.mult).then_inc(diag_ready, 1)
                dve.wait_ge(bcast_done, n)

            for k in range(PLE_KT):
                dve.wait_ge(p_hi_ready, k + 1)
                nc.vector.tensor_tensor(p_lo[:, k, :], p_raw[:, k, :], p_hi[:, k, :].bitcast(F32), ALU.subtract).then_inc(p_lo_ready, 1)
            nc.vector.memset(u[:, 0:PAD], 0.0).then_inc(conv_done, 1)
            for k in range(KT):
                dve.wait_ge(sq_ready, k + 1)
                sq = (tanh_t, work)[k % 2]
                if k == 0:
                    nc.vector.tensor_copy(sums[:], sq[:]).then_inc(sq_used, 1)
                else:
                    dve.wait_ge(sq_used, k)
                    nc.vector.tensor_tensor(sums[:], sums[:], sq[:], ALU.add).then_inc(sq_used, 1)
            dve.wait_ge(consts_loaded, 16 * 5)
            taps = cols[:, COL_TAPS:COL_TAPS + KT * TAPS]
            own.step(nc.vector.tensor_scalar(taps, taps, 0.5, None, ALU.mult))
            own.step(nc.vector.tensor_scalar(half_g[:], cols[:, COL["ln_g"]:COL["ln_g"] + KT], 0.5, None, ALU.mult))
            own.step(nc.vector.tensor_scalar(half_b[:], cols[:, COL["ln_b"]:COL["ln_b"] + KT], 0.5, None, ALU.mult))
            variance(1)
            dve.wait_ge(pos_loaded, 16)
            own.step(nc.vector.tensor_copy(v_t[:], k_raw[:].bitcast(I32)))
            own.wait()
            own.step(nc.vector.tensor_scalar(cos_t[:], v_t[:], cols[:, COL_INV:COL_INV + 1], None, ALU.mult))
            own.wait()
            own.step(nc.vector.tensor_scalar(sin_t[:], cos_t[:], 0.15915494309189535, MAGIC, ALU.mult, ALU.add))
            own.wait()
            own.step(nc.vector.tensor_scalar(sin_t[:], sin_t[:], MAGIC, None, ALU.subtract))
            for part in TWO_PI:
                own.wait()
                own.step(stt(cos_t[:], sin_t[:], -part, cos_t[:], ALU.mult, ALU.add))
            own.wait()
            nc.vector.tensor_scalar(cos_t[:], cos_t[:], 3.1415925, -3.1415925, ALU.min, ALU.max).then_inc(ang_ready, 1)
            diagonal(1)
            for k in range(KT + 1):
                if k < KT:
                    stt(conv[:, k, :], conv[:, k, :], col("ln_pre", k), banks01, ALU.mult, ALU.mult).then_inc(full_ready, 1)
                if k > 0:
                    split_low(h_lo, h_hi, k - 1, conv[:, k - 1, :], k)
            dve.wait_ge(sin_ready, 1)
            own.step(nc.vector.tensor_scalar(sin_t[:], sin_t[:], cols[:, COL_SGN:COL_SGN + 1], None, ALU.mult))
            own.step(nc.vector.tensor_tensor(cos_t[:], v_t[:], v_t[:], ALU.mult))
            own.wait()
            nc.vector.tensor_scalar(cos_t[:], cos_t[:], -2.0, 1.0, ALU.mult, ALU.add).then_inc(trig_ready, 1)

            with dve.Fori(0, KT) as i:
                own.enter(i, TAPS)
                product_done(i * 2, 1)
                dve.wait_ge(ps_free[0], i * 2 + 5)
                dve.wait_ge(conv_done, i + 1)
                stt(u[:, PAD:], tanh_t[:], 1.0, psg[:, 1, :], ALU.add, ALU.mult).then_inc(ps_free[1], 1)
                dve.wait_ge(ps_free[1], i * 2 + 5)
                def tap(j):
                    return cols[:, bass.ds(i * TAPS + (COL_TAPS + j), 1)]

                acc = conv[:, i, :]
                own.step(nc.vector.tensor_scalar(acc, u[:, 0:S], tap(0), cols[:, bass.ds(i + COL["b_dw"], 1)], ALU.mult, ALU.add))
                own.step(nc.vector.tensor_scalar(work[:], u[:, 1:1 + S], tap(1), None, ALU.mult))
                for j in range(2, TAPS):
                    dst = (acc, work[:])[j % 2]
                    dve.wait_ge(vec, own.base + own.n - 1)
                    own.step(stt(dst, u[:, j:j + S], tap(j), dst, ALU.mult, ALU.add))
                own.wait()
                nc.vector.tensor_tensor(acc, acc, work[:], ALU.add).then_inc(conv_done, 1)
            own.leave(KT)

            swap = [p ^ 8 if p < 16 else p for p in range(32)]

            def rope(t, slot, count, free):
                dve.wait_ge(qk_raw, count)
                dve.wait_ge(trig_ready, 1)
                dve.nop(nofuse=True)
                nc.vector.stream_shuffle(rtmp[:], psg[:, slot, :], swap).then_inc(ps_free[slot], 1)
                dve.wait_ge(ps_free[slot], free)
                own.step(nc.vector.tensor_tensor(rtmp[:], rtmp[:], sin_t[:], ALU.mult))
                own.step(nc.vector.tensor_tensor(t, t, cos_t[:], ALU.mult))
                own.wait()
                nc.vector.tensor_tensor(t, t, rtmp[:], ALU.add).then_inc(rope_done, 1)

            rope(k_raw[:], 0, 1, K_TILE // 2 + 5)
            with dve.Fori(0, KT // 2) as i:
                own.enter(i, 4)
                for j in range(2):
                    dve.wait_ge(rope_done, i * 2 + (j + 1))
                    rope(qo[:, i * 2 + j, :], j, i * 2 + (j + 2), i + (Q0 // 2 + 5))
                dve.wait_ge(mean_done, 1)
                for j in range(2):
                    c = i * 2 + j
                    stt(conv[:, c, :], banks01, -1.0 / D, conv[:, c, :], ALU.mult, ALU.add).then_inc(centred, 1)
            own.leave(KT // 2)

            def heads(ap, n):
                return ap.rearrange("p (a q) -> p a q", a=1).to_broadcast([P, n, P])

            def attention(n, first, c2, slot):
                for gp in range(4):
                    hs = slice(4 * gp, 4 * gp + 4)
                    dve.wait_ge(cur_copied, n * 4 + (gp + 1))
                    if first:
                        stt(probs[:, hs, :], heads(upper_q[:], 4), NEG, probs[:, hs, :], ALU.mult, ALU.add).then_inc(prev_used, 1)
                    else:
                        dve.nop(nofuse=True)
                        nc.vector.copy_predicated(probs[:, hs, :], heads(upper_q[:].bitcast(U32), 4),
                                                  score_banks(gp)[:, :, 0:P]).then_inc(prev_used, 1)
                    dve.wait_ge(prev_used, n * 4 + (gp + 1))
                    own.step(nc.vector.tensor_reduce(smax[:, hs], probs[:, hs, :], AX_X, ALU.max))
                    if gp % 2 == 1:
                        g8 = slice(8 * (gp // 2), 8 * (gp // 2) + 8)
                        own.wait()
                        own.step(stt(smax[:, g8], smax[:, g8], SCALE, sinks[:, g8], ALU.mult, ALU.max))
                        own.wait()
                        own.step(nc.vector.tensor_scalar(nmax[:, g8], smax[:, g8], -1.0, None, ALU.mult))
                        own.wait()
                        nc.vector.tensor_tensor(esink[:, g8], sinks[:, g8], smax[:, g8], ALU.subtract).then_inc(max_ready, 1)
                for g in range(2):
                    g8 = slice(8 * g, 8 * g + 8)
                    dve.wait_ge(exp_done, n * 2 + (g + 1))
                    own.step(nc.vector.tensor_tensor(denom[:, g8], denom[:, g8], esink[:, g8], ALU.add))
                    own.wait()
                    own.step(nc.vector.reciprocal(rden[:, g8], denom[:, g8]))
                    own.wait()
                    nc.vector.tensor_tensor(probs[:, g8, :], probs[:, g8, :],
                                            rden[:, g8].rearrange("p (h a) -> p h a", a=1).to_broadcast([P, 8, P]),
                                            ALU.mult).then_inc(probs_ready, 1)
                for gp in range(4):
                    dve.wait_ge(turned, n * 4 + (gp + 1))
                    if gp >= 2 or not first:
                        dve.wait_ge(pv_done, n * 4 + (gp - 1))
                    ps = psb[:, gp % 2, :].rearrange("p (j q) -> p j q", j=4)
                    prev = pt_prev[:, gp % 2, :].rearrange("p (j q) -> p j q", j=4)
                    cur = pt_cur[:, gp % 2, :].rearrange("p (j q) -> p j q", j=4)
                    own.step(nc.vector.tensor_tensor(prev, ps, heads(upper[:], 4), ALU.mult))
                    own.wait()
                    nc.vector.tensor_tensor(cur, ps, prev, ALU.subtract).then_inc(pt_ready, 1)
                dve.wait_ge(tanh_ready, n + 1)
                dve.wait_ge(spilled[slot], (c2 - C0 // 2) * 16 + 16 * 12)
                if first:
                    dve.wait_ge(var_summed, KT + 1)
                stt(ring[:, slot, :], tanh_t[:], 1.0, psg[:, slot, :], ALU.add, ALU.mult).then_inc(ps_free[slot], 1)

            c2 = C0 // 2
            attention(0, True, c2, 0)
            variance(2)
            attention(1, False, c2, 1)
            dve.wait_ge(ps_free[1], c2 + 5)
            diagonal(2)
            nc.vector.tensor_copy(sums[:], banks01).then_inc(rb_ready, 1)
            dve.wait_ge(rb_ready, 1)
            with dve.Fori(1, NB // 2) as i:
                own.enter(i, 2 * 16, 1)
                attention(i * 2, False, i + c2, 0)
                attention(i * 2 + 1, False, i + c2, 1)
            own.leave(NB // 2 - 1)

            own.wait()
            dve.sem_inc(ln_full, 1)
            with dve.Fori(0, KT // 2) as i:
                own.enter(i, 2)
                a2 = i + D0 // 2
                for j in range(2):
                    m = i * 2 + j
                    nc.vector.tensor_tensor(conv[:, m, :], conv[:, m, :], sums[:], ALU.mult).then_inc(ln_scaled, 1)
                    dve.wait_ge(ln_tanh, m + 1)
                    own.step(nc.vector.tensor_scalar(conv[:, m, :], conv[:, m, :], cols[:, bass.ds(m + COL["ln_g"], 1)],
                                                     cols[:, bass.ds(m + COL["ln_b"], 1)], ALU.mult, ALU.add))
                    own.wait()
                    stt(conv[:, m, :], ring[:, j, :], 1.0, conv[:, m, :], ALU.add, ALU.mult).then_inc(ln_full, 1)
                    dve.wait_ge(tanh_ready, m + (KT + 1))
                    stt(work[:], tanh_t[:], 1.0, psg[:, j, :], ALU.add, ALU.mult).then_inc(ps_free[j], 1)
                    dve.wait_ge(ps_free[j], i + (D0 // 2 + 5))
                    nc.vector.tensor_tensor(qo[:, m, :], qo[:, m, :], work[:], ALU.mult).then_inc(full_ready, 1)
                    split_low(o_lo, o_hi, m, qo[:, m, :], m + (KT + 1), 0.5)
            own.leave(KT // 2)

            def gate(a2, j, r):
                product_done(a2, j)
                dve.wait_ge(gate_loaded[j], r * 16)

            with dve.Fori(0, KT // 2) as i:
                for j in range(2):
                    m = i * 2 + j
                    split_low(c_lo, c_hi, m, conv[:, m, :], m + (2 * KT + 1), 0.5)
                    gate(i + E0 // 2, j, i + 1)
                    stt(merged[:, m, :], ring[:, j, :], 1.0, psg[:, j, :], ALU.add, ALU.mult).then_inc(ps_free[j], 1)
            with dve.Fori(0, KT // 2) as i:
                for j in range(2):
                    m = i * 2 + j
                    gate(i + F0 // 2, j, i + 5)
                    dve.wait_ge(lo_ready, m + 3 * KT)
                    nc.vector.tensor_tensor(work[:], psg[:, j, :], ring[:, j, :], ALU.mult).then_inc(ps_free[j], 1)
                    split_low(y_lo, y_hi, m, work[:], m + (3 * KT + 1), 0.5)
            with dve.Fori(0, KT // 2) as i:
                for j in range(2):
                    m = i * 2 + j
                    gate(i + G0 // 2, j, i + 9)
                    dve.wait_ge(full_ready, m + 2 * KT)
                    stt(work[:], ring[:, j, :], 1.0, psg[:, j, :], ALU.add, ALU.mult).then_inc(ps_free[j], 1)
                    dve.wait_ge(ps_free[j], i + (G0 // 2 + 5))
                    nc.vector.tensor_tensor(merged[:, m, :], merged[:, m, :], work[:], ALU.add).then_inc(full_ready, 1)
                    split_low(m_lo, m_hi, m, merged[:, m, :], m + (4 * KT + 1), 0.5)
            own.step(nc.vector.memset(sums[:], 0.0))
            own.wait()

            def add_square(a2, j, m, h):
                half = slice(h * HALF, (h + 1) * HALF)
                dve.wait_ge(ps_free[j], a2 + 5)
                dve.wait_ge(sq_used, m + (h + 1) * KT)
                nc.vector.tensor_tensor(sums[:, half], sums[:, half], square[:], ALU.add).then_inc(sq_used, 1)

            def x1_full(h, k):
                half = slice(h * HALF, (h + 1) * HALF)
                own.step(stt(wout[:, k, half], wout[:, k, half], col("ln_post", k), psb[:, h, :], ALU.mult, ALU.mult))
                own.wait()
                dve.wait_ge(x_again[k % 2], 16 * (4 * h + k // 2 + 1))
                nc.vector.tensor_tensor(wout[:, k, half], wout[:, k, half], ring_h[:, 0, k % 2, :], ALU.add).then_inc(full_ready, 1)

            def x1_low(h, k):
                half = slice(h * HALF, (h + 1) * HALF)
                dve.wait_ge(hi_ready, (5 + h) * KT + k + 1)
                nc.vector.tensor_tensor(x1_lo[:, k, half], wout[:, k, half], x1_hi[:, k, half].bitcast(F32),
                                        ALU.subtract).then_inc(lo_ready, 1)

            def two_x1(h, m):
                x1_full(h, 2 * m - 6)
                x1_full(h, 2 * m - 5)
                x1_low(h, 2 * m - 6)
                x1_low(h, 2 * m - 5)

            def gate_tile(a2, j, m, h):
                half = slice(h * HALF, (h + 1) * HALF)
                dve.wait_ge(ps_free[j], a2 + 5)
                dve.wait_ge(ple_loaded[j], (a2 - (I0 // 2 - 1)) * 16)
                dve.wait_ge(out_ready, m + (h * KT + 1))
                stt(square[:], tanh_h[:], 1.0, ring_h[:, 1, j, :], ALU.add, ALU.mult).then_inc(tanh_used, 1)
                dve.wait_ge(tanh_used, m + (h * KT + 2))
                stt(result[:, m, half], square[:], 0.5, wout[:, m, half], ALU.mult, ALU.add).then_inc(out_ready, 1)

            with dve.Fori(0, KT // 2) as i:
                for j in range(2):
                    add_square(i + H0 // 2, j, i * 2 + j, 0)
            for m in range(KT):
                add_square((H0 + KT + m) // 2, m % 2, m, 1)
                if m == 1:
                    variance(3, slice(0, NB // 2))
                if m == 3:
                    diagonal(3, slice(0, NB // 2))
                if 3 <= m < 7:
                    two_x1(0, m)
            dve.wait_ge(sq_used, 3 * KT)
            dve.sem_inc(tanh_used, 1)
            dve.sem_inc(out_ready, 1)
            for m in range(KT):
                gate_tile((I0 + m) // 2, m % 2, m, 0)
                if m == 1:
                    variance(4, slice(NB // 2, NB))
                if m == 3:
                    diagonal(4, slice(NB // 2, NB))
                if 3 <= m < 7:
                    two_x1(1, m)
            with dve.Fori(0, KT // 2) as i:
                for j in range(2):
                    gate_tile(i + (I0 + KT) // 2, j, i * 2 + j, 1)


SHAPES = {"xT": [P, KT, S], "pT": [P, PLE_KT, S], "weights": [P, PLE_STEPS + WTILES, KT * P], "cols": [P, NCOL],
          "masks": [P, 3, P], "positions": [P, S], "sinks_b": [P, HEADS]}


def kernel(x, p, positions, w_in, ln_pre, ln_post, w_dw, b_dw, conv_ln_g, conv_ln_b,
           w_pw, sinks, w_br_conv, w_br_attn, w_out, w_ple_gate, w_ple_proj):
    import numpy as np
    import concourse.bacc as bacc
    from concourse.bass_utils import run_bass_kernel_spmd

    def k_major(w):
        k, n = w.shape
        return w.reshape(k // P, P, n // P, P).transpose(1, 2, 0, 3).reshape(P, n // P, (k // P) * P)

    w_in = k_major(np.asarray(w_in)[0])
    val, glu, cgate, q, k, v, agate, gconv, gattn = np.split(w_in, np.cumsum([8, 8, 8, 8, 1, 1, 8, 8]), axis=1)
    first = np.stack([glu, val, gconv, gattn], axis=2).reshape(P, 4 * KT, KT * P)
    ple = k_major(np.asarray(w_ple_proj)[0]).reshape(P, PLE_STEPS, KT * P)
    weights = np.concatenate([ple, first, k, v, q, cgate, agate] +
                             [k_major(np.asarray(w)[0]) for w in (w_br_attn, w_pw, w_br_conv, w_out, w_ple_gate)], axis=1)
    per_tile = lambda a: np.asarray(a)[0].reshape(KT, P).T
    taps = np.asarray(w_dw)[0].reshape(TAPS, KT, P).transpose(2, 1, 0).reshape(P, KT * TAPS)
    dim = np.arange(P) % HD
    inv = np.where(dim < 16, (500000.0 ** (-(dim % 8) / 8.0)), 0.0).astype(np.float32)
    sgn = np.where(dim < 8, -1.0, 1.0).astype(np.float32)
    cols = np.concatenate([per_tile(a) for a in (ln_pre, ln_post, conv_ln_g, conv_ln_b, b_dw)] +
                          [taps, inv[:, None], sgn[:, None]], axis=1)
    part, free = np.arange(P)[:, None], np.arange(P)[None, :]
    masks = np.stack([part == free, part > free, free > part], axis=1).astype(np.float32)
    order = [2 * (4 * g + j) + par for g in range(2) for par in range(2) for j in range(4)]
    arrays = {
        "xT": np.asarray(x)[0].T.reshape(KT, P, S).transpose(1, 0, 2),
        "pT": np.asarray(p)[0, 0].T.reshape(PLE_KT, P, S).transpose(1, 0, 2),
        "weights": weights, "cols": cols, "masks": masks,
        "positions": np.broadcast_to(np.asarray(positions), (P, S)),
        "sinks_b": np.broadcast_to(np.asarray(sinks)[0][order], (P, HEADS)),
    }
    arrays = {n: np.ascontiguousarray(a) for n, a in arrays.items()}
    nc = bacc.Bacc("TRN2", target_bir_lowering=False, num_devices=1)
    dram = {n: nc.dram_tensor(n, SHAPES[n], mybir.dt.from_np(a.dtype), kind="ExternalInput").ap() for n, a in arrays.items()}
    dram["gates"] = nc.dram_tensor("gates", [P, 3 * KT, S], F32, kind="Internal").ap()
    dram["ple"] = nc.dram_tensor("ple", [P, KT, S], F32, kind="Internal").ap()
    dram["outT"] = nc.dram_tensor("outT", [P, KT, S], F32, kind="ExternalOutput").ap()
    build(nc, dram)
    r = run_bass_kernel_spmd(nc, [arrays], core_ids=[0])
    out = r.results[0]["outT"]
    return out.transpose(1, 0, 2).reshape(D, S).T[None]
```

```python
from contextlib import ExitStack

import concourse.bass as bass
from concourse import mybir

F32 = mybir.dt.float32
F32R = mybir.dt.float32r
I32 = mybir.dt.int32
U32 = mybir.dt.uint32
ALU = mybir.AluOpType
ACT = mybir.ActivationFunctionType
AX_X = mybir.AxisListType.X

P = 128
D = 1024
S = 1024
KT = D // P
HALF = 512
PLE_KT = 2
TAPS = 31
PAD = TAPS - 1
HEADS = 16
NB = S // P
HD = 64
EPS = 1e-6
SCALE = HD ** -0.5
NEG = -3.0e38
MAGIC = 12582912.0
TWO_PI = (6.28125, 0.0019350051879882812, 3.0199159819567e-07)

A0 = 0
K_TILE, V_TILE = 32, 33
Q0 = 34
C0 = 42
D0 = 50
E0 = 58
F0 = 66
G0 = 74
H0 = 82
I0 = 98
TILES = 114
WTILES = 98
PLE_STEPS = 2

COL = {name: 8 * j for j, name in enumerate(("ln_pre", "ln_post", "ln_g", "ln_b", "b_dw"))}
COL_TAPS = 40
COL_INV = COL_TAPS + KT * TAPS
COL_SGN = COL_INV + 1
NCOL = COL_SGN + 1


def build(nc, dram):
    with ExitStack() as ctx:
        def sem(name):
            return ctx.enter_context(nc.semaphore(name))

        KB = 1024
        start = (nc.sbuf_base + 31) // 32 * 32
        RA, RB, RC, RD, RE = (start + 32 * KB * j for j in range(5))
        W = start + 160 * KB
        G = W + 24 * KB

        def at(name, shape, dt, offset):
            return nc.alloc_sbuf_tensor_at(name, [P] + shape, dt, offset=offset)

        h_hi = at("h_hi", [KT, S], F32R, RA)
        h_lo = at("h_lo", [KT, S], F32R, RB)
        ple_out = at("ple_out", [KT, S], F32, RB)
        conv = at("conv", [KT, S], F32, RC)
        qo = at("qo", [KT, S], F32, RD)
        p_raw = at("p_raw", [PLE_KT, S], F32, RD)
        p_hi = at("p_hi", [PLE_KT, S], F32R, RD + 8 * KB)
        p_lo = at("p_lo", [PLE_KT, S], F32R, RD + 16 * KB)
        u_off = RD + 24 * KB
        u = at("u", [PAD + S], F32, u_off)
        kdup = at("kdup", [2, S], F32, RE)
        vkeys = at("vkeys", [NB, P], F32, RE + 8 * KB)
        cos_t = at("cos_t", [S], F32, RE + 12 * KB)
        sin_t = at("sin_t", [S], F32, RE + 16 * KB)
        rtmp = at("rtmp", [S], F32, RE + 20 * KB)
        v_t = at("v_t", [S], F32, RE + 24 * KB)
        k_raw = at("k_raw", [S], F32, RE + 28 * KB)
        probs = at("probs", [HEADS, P], F32, RE + 12 * KB)
        pt_cur = at("pt_cur", [2, HALF], F32, RE + 20 * KB)
        pt_prev = at("pt_prev", [2, HALF], F32, RE + 24 * KB)
        kblk = at("kblk", [2, 2 * P], F32, RE + 28 * KB)
        vblk = at("vblk", [2, P], F32, RE + 30 * KB)
        o_hi = at("o_hi", [KT, S], F32R, RE)
        o_lo = at("o_lo", [KT, S], F32R, RD)
        merged = at("merged", [KT, S], F32, RA)
        c_hi = at("c_hi", [KT, S], F32R, RB)
        c_lo = at("c_lo", [KT, S], F32R, RC)
        y_hi = at("y_hi", [KT, S], F32R, RE)
        y_lo = at("y_lo", [KT, S], F32R, RD)
        m_hi = at("m_hi", [KT, S], F32R, RB)
        m_lo = at("m_lo", [KT, S], F32R, RA)
        wout = at("wout", [KT, S], F32, RC)
        x1_hi = at("x1_hi", [KT, S], F32R, RE)
        x1_lo = at("x1_lo", [KT, S], F32R, RD)
        result = at("result", [KT, S], F32, RA)

        w_raw = at("w_raw", [2, KT * P], F32, W)
        w_hi = at("w_hi", [2, KT * P], F32R, W + 8 * KB)
        w_lo = at("w_lo", [2, KT * P], F32R, W + 16 * KB)

        tanh_t = at("tanh_t", [S], F32, G)
        diag = at("diag", [NB, P], F32, G)
        tanh_h = at("tanh_h", [HALF], F32, G + 2 * KB)
        ring_h = at("ring_h", [2, 2, HALF], F32, G + 4 * KB)
        ring = at("ring", [2, S], F32, G + 4 * KB)
        work = at("work", [S], F32, G + 12 * KB)
        square = at("square", [HALF], F32, G + 14 * KB)
        q_blk = at("q_blk", [KT, P], F32, G + 12 * KB)
        sums = at("sums", [S], F32, G + 16 * KB)
        ident = at("ident", [P], F32, G + 20 * KB)
        ones = at("ones", [P], F32, G + 20 * KB + 512)
        upper = at("upper", [P], F32, G + 21 * KB)
        upper_q = at("upper_q", [P], F32, G + 21 * KB + 512)
        cols = at("cols", [NCOL], F32, G + 22 * KB)
        small = G + 22 * KB + 4 * ((NCOL + 7) // 8 * 8)
        names = {}
        for name, n in (("half_g", KT), ("half_b", KT), ("mean_sq", 8), ("rstd", 8), ("expo", 8), ("sinks", 16),
                        ("smax", 16), ("nmax", 16), ("esink", 16), ("denom", 16), ("rden", 16)):
            names[name] = at(name, [n], F32, small)
            small += 4 * n
        half_g, half_b, mean_sq, rstd, expo = (names[n] for n in ("half_g", "half_b", "mean_sq", "rstd", "expo"))
        sinks, smax, nmax, esink, denom, rden = (names[n] for n in ("sinks", "smax", "nmax", "esink", "denom", "rden"))
        assert small <= nc.sbuf_usable_end

        psg = ctx.enter_context(nc.psum_tensor("psg", [P, 2, S], F32))
        psb = ctx.enter_context(nc.psum_tensor("psb", [P, 4, HALF], F32))

        consts_loaded = sem("consts_loaded")
        pos_loaded = sem("pos_loaded")
        p_loaded = [sem("p_loaded0"), sem("p_loaded1")]
        x_loaded = [sem(f"x_loaded{k}") for k in range(KT)]
        w_loaded = [sem("w_loaded0"), sem("w_loaded1")]
        w_hi_ready = sem("w_hi_ready")
        w_lo_ready = sem("w_lo_ready")
        tile_done = sem("tile_done")
        ps_free = [sem("ps_free0"), sem("ps_free1")]
        spilled = [sem("spilled0"), sem("spilled1")]
        ple_spilled = [sem(f"ple_spilled{k}") for k in range(KT)]
        gate_loaded = [sem("gate_loaded0"), sem("gate_loaded1")]
        tanh_ready = sem("tanh_ready")
        tanh_used = sem("tanh_used")
        vec = sem("vec")
        act_own = sem("act_own")
        pool_own = sem("pool_own")
        sq_made = sem("sq_made")
        trig_ready = sem("trig_ready")
        init_done = sem("init_done")
        p_hi_ready = sem("p_hi_ready")
        p_lo_ready = sem("p_lo_ready")
        ang_ready = sem("ang_ready")
        sin_ready = sem("sin_ready")
        sq_ready = sem("sq_ready")
        sq_used = sem("sq_used")
        var_summed = sem("var_summed")
        msq_done = sem("msq_done")
        msq_ready = sem("msq_ready")
        rstd_ready = sem("rstd_ready")
        diag_ready = sem("diag_ready")
        bcast_done = sem("bcast_done")
        full_ready = sem("full_ready")
        hi_ready = sem("hi_ready")
        lo_ready = sem("lo_ready")
        conv_done = sem("conv_done")
        csum_done = sem("csum_done")
        x_again = [sem("x_again0"), sem("x_again1")]
        ple_loaded = [sem("ple_loaded0"), sem("ple_loaded1")]
        qk_ready = sem("qk_ready")
        vb_ready = sem("vb_ready")
        mean_done = sem("mean_done")
        centred = sem("centred")
        qk_raw = sem("qk_raw")
        rope_done = sem("rope_done")
        k_dup = sem("k_dup")
        v_turned = sem("v_turned")
        v_ready = sem("v_ready")
        q_ready = sem("q_ready")
        scores_done = sem("scores_done")
        cur_copied = sem("cur_copied")
        prev_used = sem("prev_used")
        max_ready = sem("max_ready")
        exp_done = sem("exp_done")
        exp_own = sem("exp_own")
        probs_ready = sem("probs_ready")
        turned = sem("turned")
        pt_ready = sem("pt_ready")
        pv_done = sem("pv_done")
        o_ready = sem("o_ready")
        ln_scaled = sem("ln_scaled")
        ln_tanh = sem("ln_tanh")
        ln_full = sem("ln_full")
        out_ready = sem("out_ready")
        stored = sem("stored")

        XT, PT, WALL, COLS, CONST, POS, SINKS, OUT = (dram[n] for n in (
            "xT", "pT", "weights", "cols", "masks", "positions", "sinks_b", "outT"))
        GATES, PLE = dram["gates"], dram["ple"]

        banks01 = psb[:, 0:2, :].rearrange("p b s -> p (b s)")

        def score_banks(gp):
            return psb[:, 2 * (gp % 2):2 * (gp % 2) + 2, :].rearrange("p b (h k) -> p (b h) k", h=2)

        def col(name, k):
            return cols[:, k + COL[name]:k + COL[name] + 1]

        class Chain:
            def __init__(self, eng, s):
                self.eng, self.s, self.base, self.n = eng, s, 0, 0

            def step(self, ins):
                ins.then_inc(self.s, 1)
                self.n += 1

            def wait(self):
                self.eng.wait_ge(self.s, self.base + self.n)

            def enter(self, i, per, first=0):
                self.before, self.per = self.base + self.n, per
                self.base, self.n = (i - first) * per + self.before, 0

            def leave(self, times):
                assert self.n == self.per, (self.n, self.per)
                self.base, self.n = self.before + self.per * times, 0

        def x1_beside(m):
            return range((m - 2) * 3 // 2, min(KT, (m - 1) * 3 // 2)) if m >= 2 else ()

        block = ctx.enter_context(nc.Block())

        @block.sync
        def _(sp):
            def load_weights(step, slot, need=None):
                if need is not None:
                    sp.wait_ge(w_lo_ready, need)
                sp.dma_start(w_raw[:, slot, :], WALL[:, step, :]).then_inc(w_loaded[slot], 16)

            load_weights(0, 0)
            for k in range(PLE_KT):
                sp.dma_start(p_raw[:, k, :], PT[:, k, :]).then_inc(p_loaded[k], 16)
            for k in range(3):
                sp.dma_start(conv[:, k, :], XT[:, k, :]).then_inc(x_loaded[k], 16)
            load_weights(1, 1)
            for k in range(3, KT):
                sp.dma_start(conv[:, k, :], XT[:, k, :]).then_inc(x_loaded[k], 16)
            sp.dma_start(ident[:], CONST[:, 0, :]).then_inc(consts_loaded, 16)
            sp.dma_start(cols[:], COLS).then_inc(consts_loaded, 16)
            sp.dma_start(upper[:], CONST[:, 1, :]).then_inc(consts_loaded, 16)
            sp.dma_start(upper_q[:], CONST[:, 2, :]).then_inc(consts_loaded, 16)
            sp.dma_start(sinks[:], SINKS).then_inc(consts_loaded, 16)
            sp.dma_start(k_raw[:].bitcast(I32), POS).then_inc(pos_loaded, 16)
            with sp.Fori(0, H0 // 2) as i:
                for j in range(2):
                    load_weights(i * 2 + (PLE_STEPS + j), j, i * 2 + (j + 1))
            for first, tiles in ((H0, H0), (H0 + KT, H0), (I0, H0 + KT), (I0 + KT, H0 + KT)):
                with sp.Fori(0, KT // 2) as i:
                    for j in range(2):
                        load_weights(i * 2 + (tiles + PLE_STEPS + j), j, i * 2 + (first + j + 1))
            for h in range(2):
                with sp.Fori(0, KT) as m:
                    sp.wait_ge(out_ready, m + (KT * h + 2))
                    sp.dma_start(OUT[:, m, h * HALF:(h + 1) * HALF],
                                 result[:, m, h * HALF:(h + 1) * HALF]).then_inc(stored, 16)
            sp.wait_ge(stored, 16 * 2 * KT)

        @block.tensor
        def _(pe):
            def product(slot, rhs_hi, rhs_lo, ready=None, kts=KT, wslot=0, wk=0, halves=(0, 1), beside={}):
                for k in range(kts):
                    if k in beside:
                        beside[k]()
                    if ready is not None:
                        pe.wait_ge(lo_ready, ready + k + 1)
                    passes = ((w_hi, rhs_hi), (w_lo, rhs_hi), (w_hi, rhs_lo))
                    for n, (w, r) in enumerate(passes):
                        for h in halves:
                            mm = nc.tensor.matmul(psg[:, slot, h * HALF:(h + 1) * HALF],
                                                  w[:, wslot, (wk + k) * P:(wk + k + 1) * P],
                                                  r[:, k, h * HALF:(h + 1) * HALF],
                                                  start=(k == 0 and n == 0), stop=(k == kts - 1 and n == 2))
                mm.then_inc(tile_done, 1)

            def first_pair():
                order = [(0, 0)] + [(slot, k - slot) for k in range(1, KT - 2) for slot in range(2)]
                order += [(0, KT - 2), (0, KT - 1)] + [(1, k) for k in range(KT - 3, KT)]
                for slot, k in order:
                    if k == 0:
                        pe.wait_ge(w_lo_ready, PLE_STEPS + 1 + slot)
                        pe.wait_ge(ps_free[slot], KT // 2)
                    if slot == 0:
                        pe.wait_ge(lo_ready, k + 1)
                    for n, (w, r) in enumerate(((w_hi, h_hi), (w_lo, h_hi), (w_hi, h_lo))):
                        for h in range(2):
                            mm = nc.tensor.matmul(psg[:, slot, h * HALF:(h + 1) * HALF], w[:, slot, k * P:(k + 1) * P],
                                                  r[:, k, h * HALF:(h + 1) * HALF],
                                                  start=(k == 0 and n == 0), stop=(k == KT - 1 and n == 2))
                    if k == KT - 1:
                        mm.then_inc(tile_done, 1)

            def tile(a2, j, rhs_hi, rhs_lo, ready=None, halves=(0, 1), beside={}):
                pe.wait_ge(w_lo_ready, a2 * 2 + (j + PLE_STEPS + 1))
                pe.wait_ge(ps_free[j], a2 + 4)
                product(j, rhs_hi, rhs_lo, ready, wslot=j, halves=halves, beside=beside)

            def pairs(first, last, rhs_hi, rhs_lo, ready=None, halves=(0, 1)):
                with pe.Fori(first // 2, last // 2) as i:
                    tile(i, 0, rhs_hi, rhs_lo, ready, halves)
                    tile(i, 1, rhs_hi, rhs_lo, None, halves)

            def norm_pair(first, rhs_hi, rhs_lo, ready, half, n):
                blocks = (range(NB // 2), range(NB // 2, NB))[n - 3]
                tile(first // 2, 0, rhs_hi, rhs_lo, ready, (half,),
                     {KT - 1: lambda: mean_square(sq_used, (n - 1) * KT, blocks)})
                tile(first // 2, 1, rhs_hi, rhs_lo, None, (half,), {KT - 1: lambda: broadcast(n, (n - 3,))})

            def mean_square(ready, count, blocks=range(NB)):
                pe.wait_ge(ready, count)
                for c in blocks:
                    mm = nc.tensor.matmul(psb[:, 2, c:c + 1], sums[:, c * P:(c + 1) * P], ones[:, 0:1],
                                          start=True, stop=True)
                mm.then_inc(msq_done, 1)

            def broadcast(n, banks=(0, 1)):
                pe.wait_ge(diag_ready, n)
                dg = diag[:].rearrange("p c q -> p (c q)")
                for h, bank in enumerate(banks):
                    mm = nc.tensor.matmul(psb[:, bank, :], ones[:], dg[:, h * HALF:(h + 1) * HALF], start=True, stop=True)
                mm.then_inc(bcast_done, 1)

            pe.wait_ge(init_done, 1)
            for t in range(KT):
                if t % 4 == 0:
                    pe.wait_ge(w_lo_ready, t // 4 + 1)
                if t >= 2:
                    pe.wait_ge(ps_free[t % 2], t // 2)
                beside = {k: lambda k=k: pe.wait_ge(p_lo_ready, k + 1) for k in range(PLE_KT)} if t == 0 else {}
                product(t % 2, p_hi, p_lo, kts=PLE_KT, wslot=t // 4, wk=(t % 4) * PLE_KT, beside=beside)
                if t == 5:
                    mean_square(sq_used, KT)
                if t == 6:
                    broadcast(1)
            first_pair()
            pairs(A0 + 2, Q0, h_hi, h_lo)

            def conv_mean_and_values():
                pe.wait_ge(csum_done, KT)
                for h in range(2):
                    mm = nc.tensor.matmul(psb[:, h, :], ones[:], sums[:, h * HALF:(h + 1) * HALF], start=True, stop=True)
                mm.then_inc(mean_done, 1)
                pe.wait_ge(ps_free[1], 4 + V_TILE // 2 + 1)
                for c in range(NB):
                    mm = nc.tensor.transpose(psb[:, 2 + c // 4, (c % 4) * P:(c % 4 + 1) * P], v_t[:, c * P:(c + 1) * P], ident[:])
                mm.then_inc(v_turned, 1)

            tile(Q0 // 2, 0, h_hi, h_lo)
            tile(Q0 // 2, 1, h_hi, h_lo, beside={1: conv_mean_and_values})
            pairs(Q0 + 2, C0, h_hi, h_lo)
            pe.wait_ge(centred, KT)

            def block_stages(n, first=False):
                def scores(g):
                    if g == 0 or first:
                        pe.wait_ge(qk_ready, n * 2 + (3 if g or not first else 2))
                    for par in range(2):
                        if g == 1:
                            pe.wait_ge(prev_used, n * 4 + (par + 1))
                        elif not first and par == 0:
                            pe.wait_ge(pt_ready, n * 4)
                        elif not first:
                            pe.wait_ge(o_ready, n * 2)
                        for j in range(4):
                            rows = slice(par * HD, par * HD + HD)
                            c = j % 2 * 2 * P
                            rhs = kblk[rows, g, P:] if first else kblk[rows, g, :]
                            mm = nc.tensor.matmul(psb[:, 2 * par + j // 2, c + (P if first else 0):c + 2 * P],
                                                  q_blk[rows, 4 * g + j, :], rhs, start=True, stop=True)
                            if j == 3:
                                mm.then_inc(scores_done, 1)

                def transposes(g):
                    pe.wait_ge(probs_ready, n * 2 + (g + 1))
                    if g == 0:
                        pe.wait_ge(prev_used, n * 4 + 3)
                    else:
                        pe.wait_ge(pt_ready, n * 4 + 2)
                    for gp in (2 * g, 2 * g + 1):
                        for j in range(4):
                            mm = nc.tensor.transpose(psb[:, gp % 2, j * P:(j + 1) * P], probs[:, 4 * gp + j, :], ident[:])
                        mm.then_inc(turned, 1)

                def outputs(g):
                    pe.wait_ge(pt_ready, n * 4 + (2 * g + 2))
                    if g == 0:
                        pe.wait_ge(vb_ready, n + 1)
                    pe.wait_ge(prev_used, n * 4 + 4)
                    for part, pt in ((1, pt_cur), (0, pt_prev)):
                        if first and part == 0:
                            continue
                        for par in range(2):
                            mm = nc.tensor.matmul(psb[par * HD:(par + 1) * HD, 2 + g, :], vblk[:, part, g * HD:(g + 1) * HD],
                                                  pt[:, par, :], start=(part == 1), stop=(part == 0 or first))
                            if part == 0 or first:
                                mm.then_inc(pv_done, 1)

                return scores, transposes, outputs

            def both(*steps):
                return lambda: [step(arg) for step, arg in steps]

            def attention(n, slot, c2, second=False):
                scores, transposes, _ = block_stages(n)
                _, last_transposes, last_outputs = block_stages(n - 1, second)
                tile(c2, slot, h_hi, h_lo, beside={
                    0: both((last_outputs, 0), (last_transposes, 1)),
                    2: both((last_outputs, 1), (scores, 0), (scores, 1)),
                    6: both((transposes, 0))})

            pe.wait_ge(v_ready, 1)
            scores, transposes, _ = block_stages(0, True)
            scores(0)
            tile(C0 // 2, 0, h_hi, h_lo, beside={3: both((scores, 1)), 6: both((transposes, 0))})
            attention(1, 1, C0 // 2, True)
            with pe.Fori(1, NB // 2) as i:
                attention(i * 2, 0, i + C0 // 2)
                attention(i * 2 + 1, 1, i + C0 // 2)

            def conv_variance():
                pe.wait_ge(o_ready, 2 * NB)
                mean_square(var_summed, KT + 1)

            _, last_transposes, last_outputs = block_stages(NB - 1)
            tile(D0 // 2, 0, h_hi, h_lo, beside={
                0: both((last_outputs, 0), (last_transposes, 1)), 2: both((last_outputs, 1)),
                3: conv_variance, KT - 1: lambda: broadcast(2)})
            tile(D0 // 2, 1, h_hi, h_lo)
            pairs(D0 + 2, E0, h_hi, h_lo)
            pairs(E0, F0, o_hi, o_lo, KT)
            pairs(F0, G0, c_hi, c_lo, 2 * KT)
            pairs(G0, H0, y_hi, y_lo, 3 * KT)
            pairs(H0, H0 + KT, m_hi, m_lo, 4 * KT, (0,))
            H1, I1 = H0 + KT, I0 + KT
            norm_pair(H1, m_hi, m_lo, None, 1, 3)
            pairs(H1 + 2, I0, m_hi, m_lo, None, (1,))
            norm_pair(I0, x1_hi, x1_lo, 5 * KT, 0, 4)
            pairs(I0 + 2, I1, x1_hi, x1_lo, None, (0,))
            pairs(I1, TILES, x1_hi, x1_lo, 6 * KT, (1,))

        @block.gpsimd
        def _(pool):
            own = Chain(pool, pool_own)
            nc.gpsimd.memset(ones[:], 1.0).then_inc(init_done, 1)
            own.step(nc.gpsimd.memset(expo[:], -0.5))

            def low_part(step, slot):
                pool.wait_ge(w_hi_ready, step + 1)
                nc.gpsimd.tensor_tensor(w_lo[:, slot, :], w_raw[:, slot, :], w_hi[:, slot, :].bitcast(F32),
                                        ALU.subtract).then_inc(w_lo_ready, 1)

            def low(a2, j):
                low_part(a2 * 2 + (PLE_STEPS + j), j % 2)

            def rsqrt(n, c=slice(0, NB)):
                pool.wait_ge(msq_ready, n)
                own.wait()
                nc.gpsimd.tensor_tensor(rstd[:, c], mean_sq[:, c], expo[:, c], ALU.pow).then_inc(rstd_ready, 1)

            def add_conv(i):
                pool.wait_ge(conv_done, i + 2)
                pool.wait_ge(csum_done, i)
                nc.gpsimd.tensor_tensor(sums[:], sums[:], conv[:, i, :], ALU.add).then_inc(csum_done, 1)

            pool.wait_ge(w_lo_ready, 1)
            low_part(1, 1)
            rsqrt(1)
            own.step(nc.gpsimd.memset(sums[:], 0.0))
            low(0, 0)
            low(0, 1)
            low(0, 2)
            low(0, 3)
            low(0, 4)
            low(0, 5)
            pool.wait_ge(sin_ready, 1)
            own.step(nc.gpsimd.tensor_tensor(cos_t[:], v_t[:], v_t[:], ALU.mult))
            own.wait()
            nc.gpsimd.tensor_scalar(cos_t[:], cos_t[:], -2.0, 1.0, ALU.mult, ALU.add).then_inc(trig_ready, 1)
            nc.gpsimd.tensor_scalar(sin_t[:], sin_t[:], cols[:, COL_SGN:COL_SGN + 1], None, ALU.mult).then_inc(trig_ready, 1)
            with pool.Fori(1, KT) as i:
                low(i * 2, 2)
                add_conv(i - 1)
                low(i * 2, 3)
                low(i * 2, 4)
                low(i * 2, 5)
            low(Q0 // 2, 0)
            add_conv(KT - 1)
            low(Q0 // 2, 1)
            pool.wait_ge(mean_done, 1)
            nc.gpsimd.memset(sums[:], 0.0).then_inc(var_summed, 1)
            pool.wait_ge(spilled[1], 16 * 8)
            with pool.Fori(0, KT // 2) as i:
                low(i + Q0 // 2 + 1, 0)
                low(i + Q0 // 2 + 1, 1)
                for j in range(2):
                    c = i * 2 + j
                    pool.wait_ge(centred, c + 1)
                    pool.wait_ge(var_summed, c + 1)
                    nc.gpsimd.tensor_tensor(ring[:, 1, :], conv[:, c, :], conv[:, c, :], ALU.mult).then_inc(sq_made, 1)
                    pool.wait_ge(sq_made, c + 1)
                    nc.gpsimd.tensor_tensor(sums[:], sums[:], ring[:, 1, :], ALU.add).then_inc(var_summed, 1)

            def lows(first, last):
                with pool.Fori(first // 2, last // 2) as i:
                    low(i, 0)
                    low(i, 1)

            lows(Q0 + 10, D0 + 2)
            rsqrt(2)
            lows(D0 + 2, H0 + KT + 2)
            rsqrt(3, slice(0, NB // 2))
            lows(H0 + KT + 2, I0 + 2)
            rsqrt(4, slice(NB // 2, NB))
            lows(I0 + 2, TILES)

        @block.scalar
        def _(act):
            def settled():
                act.nop(nofuse=True)

            def high(a2, j):
                act.wait_ge(w_loaded[j % 2], (a2 + j // 2) * 16 + 32)
                act.wait_ge(tile_done, a2 * 2 + (j + KT - 1))
                nc.scalar.activation(w_hi[:, j % 2, :], w_raw[:, j % 2, :], ACT.Copy).then_inc(w_hi_ready, 1)

            def product_done(a2, j):
                act.wait_ge(tile_done, a2 * 2 + (j + KT + 1))

            def read_out(a2, j):
                act.wait_ge(ps_free[j], a2 + 5)

            def split_high(dst, k, src, index, scale=1.0):
                settled()
                nc.scalar.activation(dst[:, k, :], src, ACT.Copy, scale=scale).then_inc(hi_ready, 1)

            def spill(dst, slot):
                act.dma_start(dst, ring[:, slot, :]).then_inc(spilled[slot], 16)

            act.wait_ge(w_loaded[0], 16)
            nc.scalar.activation(w_hi[:, 0, :], w_raw[:, 0, :], ACT.Copy).then_inc(w_hi_ready, 1)
            for k in range(PLE_KT):
                act.wait_ge(p_loaded[k], 16)
                nc.scalar.activation(p_hi[:, k, :], p_raw[:, k, :], ACT.Copy).then_inc(p_hi_ready, 1)
            squares = (tanh_t, work)

            def read_ple(t):
                act.wait_ge(tile_done, t + 1)
                nc.scalar.activation(ple_out[:, t, :], psg[:, t % 2, :], ACT.Copy).then_inc(ps_free[t % 2], 1)

            def spill_ple(t):
                act.wait_ge(ps_free[t % 2], t // 2 + 1)
                act.dma_start(PLE[:, t, :], ple_out[:, t, :]).then_inc(ple_spilled[t], 16)

            def square_x(k):
                act.wait_ge(x_loaded[k], 16)
                if k >= 2:
                    act.wait_ge(sq_used, k - 1)
                nc.scalar.activation(squares[k % 2][:], conv[:, k, :], ACT.Square).then_inc(sq_ready, 1)

            def first_high(j, done):
                act.wait_ge(w_loaded[j], 32)
                act.wait_ge(tile_done, done)
                nc.scalar.activation(w_hi[:, j, :], w_raw[:, j, :], ACT.Copy).then_inc(w_hi_ready, 1)

            def h_high(k):
                act.wait_ge(full_ready, k + 1)
                split_high(h_hi, k, conv[:, k, :], k)

            for k in range(3):
                square_x(k)
            act.wait_ge(w_loaded[1], 16)
            nc.scalar.activation(w_hi[:, 1, :], w_raw[:, 1, :], ACT.Copy).then_inc(w_hi_ready, 1)
            square_x(3)
            read_ple(0)
            square_x(4)
            read_ple(1)
            square_x(5)
            square_x(6)
            read_ple(2)
            square_x(7)
            read_ple(3)
            first_high(0, 4)
            for t in range(4):
                spill_ple(t)
            for t in range(4, 7):
                read_ple(t)
                spill_ple(t)
            h_high(0)
            h_high(1)
            read_ple(7)
            spill_ple(7)
            first_high(1, KT)
            for k in range(2, KT):
                h_high(k)

            def glu_and_merge(i, first=False):
                a2 = i * 2
                product_done(a2, 0)
                act.wait_ge(ps_free[1], i * 2 + 3)
                nc.scalar.activation(tanh_t[:], psg[:, 0, :], ACT.Tanh, scale=0.5).then_inc(ps_free[0], 1)
                high(a2, 2)
                high(a2, 3)
                product_done(a2, 2)
                if not first:
                    act.wait_ge(spilled[0], i * 16)
                nc.scalar.activation(ring[:, 0, :], psg[:, 0, :], ACT.Tanh, scale=0.5).then_inc(ps_free[0], 1)
                act.wait_ge(ps_free[0], i * 2 + 6)
                spill(GATES[:, i + 2 * KT, :], 0)
                high(a2, 4)
                product_done(a2, 3)
                if not first:
                    act.wait_ge(spilled[1], i * 16)
                nc.scalar.activation(ring[:, 1, :], psg[:, 1, :], ACT.Tanh, scale=0.5).then_inc(ps_free[1], 1)
                act.wait_ge(ps_free[1], i * 2 + 6)
                spill(GATES[:, i, :], 1)
                high(a2, 5)

            glu_and_merge(0, True)
            act.wait_ge(ang_ready, 1)
            nc.scalar.activation(sin_t[:], cos_t[:], ACT.Sin)
            nc.scalar.activation(v_t[:], cos_t[:], ACT.Sin, scale=0.5).then_inc(sin_ready, 1)
            with act.Fori(1, KT) as i:
                glu_and_merge(i)
            product_done(K_TILE // 2, 0)
            nc.scalar.activation(k_raw[:], psg[:, 0, :], ACT.Copy).then_inc(qk_raw, 1)
            high(K_TILE // 2, 2)
            product_done(K_TILE // 2, 1)
            act.wait_ge(trig_ready, 1)
            nc.scalar.activation(v_t[:], psg[:, 1, :], ACT.Copy).then_inc(ps_free[1], 1)

            def query_pair(i):
                for j in range(2):
                    high(i + Q0 // 2, j + 1)
                    product_done(i + Q0 // 2, j)
                    if j == 0:
                        act.wait_ge(conv_done, KT + 1)
                    settled()
                    nc.scalar.activation(qo[:, i * 2 + j, :], psg[:, j, :], ACT.Copy).then_inc(qk_raw, 1)

            query_pair(0)
            act.wait_ge(rope_done, 1)
            for g in range(2):
                for half in range(2):
                    act.dma_start(kdup[half * HD:(half + 1) * HD, g, :], k_raw[g * HD:(g + 1) * HD, :]).then_inc(k_dup, 16)
            act.wait_ge(v_turned, 1)
            nc.scalar.activation(vkeys[:].rearrange("p c d -> p (c d)"), psb[:, 2:4, :].rearrange("p b s -> p (b s)"),
                                 ACT.Copy).then_inc(v_ready, 1)
            with act.Fori(1, KT // 2 - 1) as i:
                query_pair(i)
            act.wait_ge(rope_done, 1 + KT // 2)
            act.wait_ge(k_dup, 64)
            nc.scalar.activation(q_blk[:, 0:KT // 2, :], qo[:, 0:KT // 2, 0:P], ACT.Copy).then_inc(qk_ready, 1)
            nc.scalar.activation(kblk[:, :, P:], kdup[:, :, 0:P], ACT.Copy).then_inc(qk_ready, 1)
            query_pair(KT // 2 - 1)
            act.wait_ge(rope_done, 1 + KT)
            nc.scalar.activation(q_blk[:, KT // 2:, :], qo[:, KT // 2:, 0:P], ACT.Copy).then_inc(qk_ready, 1)

            def load_qk(n):
                settled()
                nc.scalar.activation(q_blk[:], qo[:, :, bass.ds(n * P, P)], ACT.Copy).then_inc(qk_ready, 1)
                settled()
                nc.scalar.activation(kblk[:], kdup[:, :, bass.ds(n * P - P, 2 * P)], ACT.Copy).then_inc(qk_ready, 1)

            def load_v(n, first=False):
                if first:
                    nc.scalar.activation(vblk[:, 1, :], vkeys[:, 0, :], ACT.Copy).then_inc(vb_ready, 1)
                else:
                    settled()
                    nc.scalar.activation(vblk[:], vkeys[:, bass.ds(n - 1, 2), :], ACT.Copy).then_inc(vb_ready, 1)

            act.wait_ge(v_ready, 1)
            load_v(0, True)

            def attention(n, first, last, c2, slot):
                def copy_scores(gp):
                    act.wait_ge(scores_done, n * 4 + (gp + 1))
                    nc.scalar.activation(probs[:, 4 * gp:4 * gp + 4, :], score_banks(gp)[:, :, P:], ACT.Copy).then_inc(cur_copied, 1)

                def exps(gp):
                    for h in range(4 * gp, 4 * gp + 4):
                        nc.scalar.activation(probs[:, h, :], probs[:, h, :], ACT.Exp, bias=nmax[:, h:h + 1], scale=SCALE,
                                             accum_out=denom[:, h:h + 1])
                    if gp % 2 == 1:
                        g8 = slice(4 * gp - 4, 4 * gp + 4)
                        nc.scalar.activation(esink[:, g8], esink[:, g8], ACT.Exp).then_inc(exp_done, 1)

                def outputs(g):
                    act.wait_ge(pv_done, n * 4 + (2 * g + 2))
                    settled()
                    nc.scalar.activation(qo[:, 4 * g:4 * g + 4, bass.ds(n * P, P)],
                                         psb[:, 2 + g, :].rearrange("p (m q) -> p m q", m=4), ACT.Copy).then_inc(o_ready, 1)

                if not first:
                    act.wait_ge(turned, n * 4)
                copy_scores(0)
                copy_scores(1)
                copy_scores(2)
                act.wait_ge(max_ready, n * 2 + 1)
                exps(0)
                copy_scores(3)
                exps(1)
                act.wait_ge(max_ready, n * 2 + 2)
                exps(2)
                exps(3)
                product_done(c2, slot)
                if not first:
                    act.wait_ge(ps_free[1 - slot], c2 + 4 + slot)
                nc.scalar.activation(tanh_t[:], psg[:, slot, :], ACT.Tanh, scale=0.5).then_inc(tanh_ready, 1)
                if not last:
                    load_qk(n + 1)
                outputs(0)
                if not last:
                    high(c2, slot + 2)
                outputs(1)
                if not last:
                    load_v(n + 1)
                read_out(c2, slot)
                spill(GATES[:, n + KT, :], slot)

            c2 = C0 // 2
            high(c2, 1)
            attention(0, True, False, c2, 0)
            attention(1, False, False, c2, 1)
            with act.Fori(1, NB // 2 - 1) as i:
                attention(i * 2, False, False, i + c2, 0)
                attention(i * 2 + 1, False, False, i + c2, 1)
            attention(NB - 2, False, False, c2 + NB // 2 - 1, 0)
            attention(NB - 1, False, True, c2 + NB // 2 - 1, 1)

            act.wait_ge(spilled[0], 16 * 12)
            act.wait_ge(spilled[1], 16 * 12)
            with act.Fori(0, KT // 2) as i:
                a2 = i + D0 // 2
                for j in range(2):
                    m = i * 2 + j
                    high(a2, j + 1)
                    act.wait_ge(ln_scaled, m + 1)
                    act.wait_ge(ln_full, m + 1 if j == 0 else m)
                    settled()
                    nc.scalar.activation(ring[:, j, :], conv[:, m, :], ACT.Tanh, bias=half_b[:, bass.ds(m, 1)],
                                         scale=half_g[:, bass.ds(m, 1)]).then_inc(ln_tanh, 1)
                    product_done(a2, j)
                    act.wait_ge(full_ready, m + KT)
                    act.wait_ge(bcast_done, 2)
                    nc.scalar.activation(tanh_t[:], psg[:, j, :], ACT.Tanh, scale=0.5).then_inc(tanh_ready, 1)
                    act.wait_ge(full_ready, m + (KT + 1))
                    split_high(o_hi, m, qo[:, m, :], m, 0.5)
            act.wait_ge(ln_full, KT + 1)

            def load_gate(r, slot, a2):
                act.wait_ge(ps_free[slot], a2 + 4)
                act.dma_start(ring[:, slot, :], GATES[:, r, :]).then_inc(gate_loaded[slot], 16)

            with act.Fori(0, KT // 2) as i:
                a2 = i + E0 // 2
                for j in range(2):
                    m = i * 2 + j
                    high(a2, j + 1)
                    load_gate(m, j, a2)
                    if j == 0:
                        act.wait_ge(tile_done, E0 + KT)
                    split_high(c_hi, m, conv[:, m, :], m, 0.5)
            with act.Fori(0, KT // 2) as i:
                a2 = i + F0 // 2
                for j in range(2):
                    m = i * 2 + j
                    high(a2, j + 1)
                    load_gate(m + KT, j, a2)
                    read_out(a2, j)
                    split_high(y_hi, m, work[:], m, 0.5)
            with act.Fori(0, KT // 2) as i:
                a2 = i + G0 // 2
                for j in range(2):
                    m = i * 2 + j
                    high(a2, j + 1)
                    load_gate(m + 2 * KT, j, a2)
                    act.wait_ge(full_ready, m + (2 * KT + 1))
                    split_high(m_hi, m, merged[:, m, :], m, 0.5)
            high(H0 // 2, 1)

            def x_back(h, k):
                act.dma_start(ring_h[:, 0, k % 2, :], XT[:, k, h * HALF:(h + 1) * HALF]).then_inc(x_again[k % 2], 16)

            def ple_back(h, m, j):
                act.dma_start(ring_h[:, 1, j, :], PLE[:, m, h * HALF:(h + 1) * HALF]).then_inc(ple_loaded[j], 16)

            for k in range(2):
                x_back(0, k)
                ple_back(0, k, k)

            def w_out_tile(a2, j, m, h):
                half = slice(h * HALF, (h + 1) * HALF)
                product_done(a2, j)
                settled()
                nc.scalar.activation(wout[:, m, half], psg[:, j, half], ACT.Copy)
                high(a2, j + 2)
                act.wait_ge(sq_used, m + (h + 1) * KT)
                nc.scalar.activation(square[:], psg[:, j, half], ACT.Square).then_inc(ps_free[j], 1)

            def x1_high(h, k):
                half = slice(h * HALF, (h + 1) * HALF)
                act.wait_ge(full_ready, (3 + h) * KT + k + 1)
                nc.scalar.activation(x1_hi[:, k, half], wout[:, k, half], ACT.Copy).then_inc(hi_ready, 1)
                if (h, k) < (1, KT - 2):
                    x_back(h + (k + 2) // KT, (k + 2) % KT)

            def gate_tile(a2, j, m, h, more=True, again=True):
                half = slice(h * HALF, (h + 1) * HALF)
                product_done(a2, j)
                act.wait_ge(tanh_used, m + (h * KT + 1))
                if again:
                    ple_back(*again)
                nc.scalar.activation(tanh_h[:], psg[:, j, half], ACT.Tanh, scale=0.5).then_inc(ps_free[j], 1)
                if more:
                    high(a2, j + 2)

            with act.Fori(0, KT // 2) as i:
                for j in range(2):
                    w_out_tile(i + H0 // 2, j, i * 2 + j, 0)
            for m in range(KT):
                for k in x1_beside(m):
                    x1_high(0, k)
                w_out_tile((H0 + KT + m) // 2, m % 2, m, 1)
            for m in range(KT):
                for k in x1_beside(m):
                    x1_high(1, k)
                gate_tile((I0 + m) // 2, m % 2, m, 0, again=(0, m + 1, (m + 1) % 2) if 1 <= m < KT - 1
                          else (1, 0, 0) if m == KT - 1 else None)
            with act.Fori(0, KT // 2 - 1) as i:
                for j in range(2):
                    m = i * 2 + j
                    gate_tile(i + (I0 + KT) // 2, j, m, 1, again=(1, m + 1, (j + 1) % 2))
            gate_tile(TILES // 2 - 1, 0, KT - 2, 1, more=False, again=(1, KT - 1, 1))
            gate_tile(TILES // 2 - 1, 1, KT - 1, 1, more=False, again=None)

        @block.vector
        def _(dve):
            own = Chain(dve, vec)
            stt = nc.vector.scalar_tensor_tensor

            def product_done(a2, j):
                dve.wait_ge(tile_done, a2 * 2 + (j + KT + 1))

            def split_low(dst, hi, k, src, count, scale=1.0):
                dve.wait_ge(hi_ready, count)
                stt(dst[:, k, :], src, scale, hi[:, k, :].bitcast(F32), ALU.mult, ALU.subtract).then_inc(lo_ready, 1)

            def variance(n, c=slice(0, NB)):
                dve.wait_ge(msq_done, n)
                nc.vector.tensor_scalar(mean_sq[:, c], psb[:, 2, c], 1.0 / D, EPS, ALU.mult, ALU.add).then_inc(msq_ready, 1)

            def diagonal(n, c=slice(0, NB)):
                k = c.stop - c.start
                dve.wait_ge(rstd_ready, n)
                nc.vector.tensor_tensor(diag[:, 0:k, :], ident[:].rearrange("p (a q) -> p a q", a=1).to_broadcast([P, k, P]),
                                        rstd[:, c].rearrange("p (c a) -> p c a", a=1).to_broadcast([P, k, P]),
                                        ALU.mult).then_inc(diag_ready, 1)

            dve.wait_ge(w_hi_ready, 1)
            nc.vector.tensor_tensor(w_lo[:, 0, :], w_raw[:, 0, :], w_hi[:, 0, :].bitcast(F32), ALU.subtract).then_inc(w_lo_ready, 1)
            for k in range(PLE_KT):
                dve.wait_ge(p_hi_ready, k + 1)
                nc.vector.tensor_tensor(p_lo[:, k, :], p_raw[:, k, :], p_hi[:, k, :].bitcast(F32), ALU.subtract).then_inc(p_lo_ready, 1)
            nc.vector.memset(u[:, 0:PAD], 0.0).then_inc(conv_done, 1)
            for k in range(KT):
                dve.wait_ge(sq_ready, k + 1)
                sq = (tanh_t, work)[k % 2]
                if k == 0:
                    nc.vector.tensor_copy(sums[:], sq[:]).then_inc(sq_used, 1)
                else:
                    dve.wait_ge(sq_used, k)
                    nc.vector.tensor_tensor(sums[:], sums[:], sq[:], ALU.add).then_inc(sq_used, 1)
            dve.wait_ge(consts_loaded, 16 * 5)
            taps = cols[:, COL_TAPS:COL_TAPS + KT * TAPS]
            own.step(nc.vector.tensor_scalar(taps, taps, 0.5, None, ALU.mult))
            own.step(nc.vector.tensor_scalar(half_g[:], cols[:, COL["ln_g"]:COL["ln_g"] + KT], 0.5, None, ALU.mult))
            own.step(nc.vector.tensor_scalar(half_b[:], cols[:, COL["ln_b"]:COL["ln_b"] + KT], 0.5, None, ALU.mult))
            variance(1)
            diagonal(1)
            dve.wait_ge(bcast_done, 1)
            for k in range(KT + 1):
                if k < KT:
                    stt(conv[:, k, :], conv[:, k, :], col("ln_pre", k), banks01, ALU.mult, ALU.mult).then_inc(full_ready, 1)
                if k > 0:
                    dve.wait_ge(ple_spilled[k - 1], 16)
                    split_low(h_lo, h_hi, k - 1, conv[:, k - 1, :], k)

            dve.wait_ge(pos_loaded, 16)
            own.step(nc.vector.tensor_copy(v_t[:], k_raw[:].bitcast(I32)))
            own.wait()
            own.step(nc.vector.tensor_scalar(cos_t[:], v_t[:], cols[:, COL_INV:COL_INV + 1], None, ALU.mult))
            own.wait()
            own.step(nc.vector.tensor_scalar(sin_t[:], cos_t[:], 0.15915494309189535, MAGIC, ALU.mult, ALU.add))
            own.wait()
            own.step(nc.vector.tensor_scalar(sin_t[:], sin_t[:], MAGIC, None, ALU.subtract))
            for part in TWO_PI:
                own.wait()
                own.step(stt(cos_t[:], sin_t[:], -part, cos_t[:], ALU.mult, ALU.add))
            own.wait()
            nc.vector.tensor_scalar(cos_t[:], cos_t[:], 3.1415925, -3.1415925, ALU.min, ALU.max).then_inc(ang_ready, 1)

            with dve.Fori(0, KT) as i:
                own.enter(i, TAPS)
                product_done(i * 2, 1)
                dve.wait_ge(ps_free[0], i * 2 + 5)
                dve.wait_ge(conv_done, i + 1)
                stt(u[:, PAD:], tanh_t[:], 1.0, psg[:, 1, :], ALU.add, ALU.mult).then_inc(ps_free[1], 1)
                dve.wait_ge(ps_free[1], i * 2 + 5)
                def tap(j):
                    return cols[:, bass.ds(i * TAPS + (COL_TAPS + j), 1)]

                acc = conv[:, i, :]
                own.step(nc.vector.tensor_scalar(acc, u[:, 0:S], tap(0), cols[:, bass.ds(i + COL["b_dw"], 1)], ALU.mult, ALU.add))
                own.step(nc.vector.tensor_scalar(work[:], u[:, 1:1 + S], tap(1), None, ALU.mult))
                for j in range(2, TAPS):
                    dst = (acc, work[:])[j % 2]
                    dve.wait_ge(vec, own.base + own.n - 1)
                    own.step(stt(dst, u[:, j:j + S], tap(j), dst, ALU.mult, ALU.add))
                own.wait()
                nc.vector.tensor_tensor(acc, acc, work[:], ALU.add).then_inc(conv_done, 1)
            own.leave(KT)

            swap = [p ^ 8 if p < 16 else p for p in range(32)]

            def rope(t, slot, count, free):
                dve.wait_ge(qk_raw, count)
                dve.wait_ge(trig_ready, 2)
                dve.nop(nofuse=True)
                nc.vector.stream_shuffle(rtmp[:], psg[:, slot, :], swap).then_inc(ps_free[slot], 1)
                dve.wait_ge(ps_free[slot], free)
                own.step(nc.vector.tensor_tensor(rtmp[:], rtmp[:], sin_t[:], ALU.mult))
                own.step(nc.vector.tensor_tensor(t, t, cos_t[:], ALU.mult))
                own.wait()
                nc.vector.tensor_tensor(t, t, rtmp[:], ALU.add).then_inc(rope_done, 1)

            rope(k_raw[:], 0, 1, K_TILE // 2 + 5)
            with dve.Fori(0, KT // 2) as i:
                own.enter(i, 4)
                dve.wait_ge(mean_done, 1)
                for j in range(2):
                    c = i * 2 + j
                    stt(conv[:, c, :], banks01, -1.0 / D, conv[:, c, :], ALU.mult, ALU.add).then_inc(centred, 1)
                for j in range(2):
                    dve.wait_ge(rope_done, i * 2 + (j + 1))
                    rope(qo[:, i * 2 + j, :], j, i * 2 + (j + 2), i + (Q0 // 2 + 5))
            own.leave(KT // 2)

            def heads(ap, n):
                return ap.rearrange("p (a q) -> p a q", a=1).to_broadcast([P, n, P])

            def attention(n, first, c2, slot):
                def maxima(gp):
                    hs = slice(4 * gp, 4 * gp + 4)
                    dve.wait_ge(cur_copied, n * 4 + (gp + 1))
                    if first:
                        stt(probs[:, hs, :], heads(upper_q[:], 4), NEG, probs[:, hs, :], ALU.mult, ALU.add).then_inc(prev_used, 1)
                    else:
                        dve.nop(nofuse=True)
                        nc.vector.copy_predicated(probs[:, hs, :], heads(upper_q[:].bitcast(U32), 4),
                                                  score_banks(gp)[:, :, 0:P]).then_inc(prev_used, 1)
                    dve.wait_ge(prev_used, n * 4 + (gp + 1))
                    own.step(nc.vector.tensor_reduce(smax[:, hs], probs[:, hs, :], AX_X, ALU.max))
                    if gp % 2 == 1:
                        g8 = slice(8 * (gp // 2), 8 * (gp // 2) + 8)
                        own.wait()
                        own.step(stt(smax[:, g8], smax[:, g8], SCALE, sinks[:, g8], ALU.mult, ALU.max))
                        own.wait()
                        own.step(nc.vector.tensor_scalar(nmax[:, g8], smax[:, g8], -1.0, None, ALU.mult))
                        own.wait()
                        nc.vector.tensor_tensor(esink[:, g8], sinks[:, g8], smax[:, g8], ALU.subtract).then_inc(max_ready, 1)

                def normalise(g):
                    g8 = slice(8 * g, 8 * g + 8)
                    dve.wait_ge(exp_done, n * 2 + (g + 1))
                    own.step(nc.vector.tensor_tensor(denom[:, g8], denom[:, g8], esink[:, g8], ALU.add))
                    own.wait()
                    own.step(nc.vector.reciprocal(rden[:, g8], denom[:, g8]))
                    own.wait()
                    nc.vector.tensor_tensor(probs[:, g8, :], probs[:, g8, :],
                                            rden[:, g8].rearrange("p (h a) -> p h a", a=1).to_broadcast([P, 8, P]),
                                            ALU.mult).then_inc(probs_ready, 1)

                def split_window(g):
                    for gp in (2 * g, 2 * g + 1):
                        dve.wait_ge(turned, n * 4 + (gp + 1))
                        if g == 1 or not first:
                            dve.wait_ge(pv_done, n * 4 + 2 * g)
                        ps = psb[:, gp % 2, :].rearrange("p (j q) -> p j q", j=4)
                        prev = pt_prev[:, gp % 2, :].rearrange("p (j q) -> p j q", j=4)
                        cur = pt_cur[:, gp % 2, :].rearrange("p (j q) -> p j q", j=4)
                        own.step(nc.vector.tensor_tensor(prev, ps, heads(upper[:], 4), ALU.mult))
                        own.wait()
                        nc.vector.tensor_tensor(cur, ps, prev, ALU.subtract).then_inc(pt_ready, 1)

                maxima(0)
                maxima(1)
                maxima(2)
                maxima(3)
                normalise(0)
                split_window(0)
                normalise(1)
                dve.wait_ge(tanh_ready, n + 1)
                dve.wait_ge(spilled[slot], (c2 - C0 // 2) * 16 + 16 * 8)
                if slot == 1:
                    dve.wait_ge(var_summed, KT + 1)
                stt(ring[:, slot, :], tanh_t[:], 1.0, psg[:, slot, :], ALU.add, ALU.mult).then_inc(ps_free[slot], 1)
                split_window(1)

            c2 = C0 // 2
            attention(0, True, c2, 0)
            attention(1, False, c2, 1)
            with dve.Fori(1, NB // 2) as i:
                own.enter(i, 2 * 16, 1)
                attention(i * 2, False, i + c2, 0)
                attention(i * 2 + 1, False, i + c2, 1)
            own.leave(NB // 2 - 1)

            own.wait()
            dve.sem_inc(ln_full, 1)
            variance(2)
            dve.wait_ge(ps_free[1], D0 // 2 + 4)
            diagonal(2)
            dve.wait_ge(bcast_done, 2)
            with dve.Fori(0, KT // 2) as i:
                own.enter(i, 2)
                a2 = i + D0 // 2
                for j in range(2):
                    m = i * 2 + j
                    nc.vector.tensor_tensor(conv[:, m, :], conv[:, m, :], banks01, ALU.mult).then_inc(ln_scaled, 1)
                    dve.wait_ge(ln_tanh, m + 1)
                    own.step(nc.vector.tensor_scalar(conv[:, m, :], conv[:, m, :], cols[:, bass.ds(m + COL["ln_g"], 1)],
                                                     cols[:, bass.ds(m + COL["ln_b"], 1)], ALU.mult, ALU.add))
                    own.wait()
                    stt(conv[:, m, :], ring[:, j, :], 1.0, conv[:, m, :], ALU.add, ALU.mult).then_inc(ln_full, 1)
                    dve.wait_ge(tanh_ready, m + (KT + 1))
                    stt(work[:], tanh_t[:], 1.0, psg[:, j, :], ALU.add, ALU.mult).then_inc(ps_free[j], 1)
                    dve.wait_ge(ps_free[j], i + (D0 // 2 + 5))
                    nc.vector.tensor_tensor(qo[:, m, :], qo[:, m, :], work[:], ALU.mult).then_inc(full_ready, 1)
                    split_low(o_lo, o_hi, m, qo[:, m, :], m + (KT + 1), 0.5)
            own.leave(KT // 2)

            def gate(a2, j, r):
                product_done(a2, j)
                dve.wait_ge(gate_loaded[j], r * 16)

            with dve.Fori(0, KT // 2) as i:
                for j in range(2):
                    m = i * 2 + j
                    split_low(c_lo, c_hi, m, conv[:, m, :], m + (2 * KT + 1), 0.5)
                    gate(i + E0 // 2, j, i + 1)
                    stt(merged[:, m, :], ring[:, j, :], 1.0, psg[:, j, :], ALU.add, ALU.mult).then_inc(ps_free[j], 1)
            with dve.Fori(0, KT // 2) as i:
                for j in range(2):
                    m = i * 2 + j
                    gate(i + F0 // 2, j, i + 5)
                    dve.wait_ge(lo_ready, m + 3 * KT)
                    nc.vector.tensor_tensor(work[:], psg[:, j, :], ring[:, j, :], ALU.mult).then_inc(ps_free[j], 1)
                    split_low(y_lo, y_hi, m, work[:], m + (3 * KT + 1), 0.5)
            with dve.Fori(0, KT // 2) as i:
                for j in range(2):
                    m = i * 2 + j
                    gate(i + G0 // 2, j, i + 9)
                    dve.wait_ge(full_ready, m + 2 * KT)
                    stt(work[:], ring[:, j, :], 1.0, psg[:, j, :], ALU.add, ALU.mult).then_inc(ps_free[j], 1)
                    dve.wait_ge(ps_free[j], i + (G0 // 2 + 5))
                    nc.vector.tensor_tensor(merged[:, m, :], merged[:, m, :], work[:], ALU.add).then_inc(full_ready, 1)
                    split_low(m_lo, m_hi, m, merged[:, m, :], m + (4 * KT + 1), 0.5)
            own.step(nc.vector.memset(sums[:], 0.0))
            own.wait()

            def add_square(a2, j, m, h):
                half = slice(h * HALF, (h + 1) * HALF)
                dve.wait_ge(ps_free[j], a2 + 5)
                dve.wait_ge(sq_used, m + (h + 1) * KT)
                nc.vector.tensor_tensor(sums[:, half], sums[:, half], square[:], ALU.add).then_inc(sq_used, 1)

            def x1_full(h, k):
                half = slice(h * HALF, (h + 1) * HALF)
                dve.wait_ge(bcast_done, 3 + h)
                own.step(stt(wout[:, k, half], wout[:, k, half], col("ln_post", k), psb[:, h, :], ALU.mult, ALU.mult))
                own.wait()
                dve.wait_ge(x_again[k % 2], 16 * (4 * h + k // 2 + 1))
                nc.vector.tensor_tensor(wout[:, k, half], wout[:, k, half], ring_h[:, 0, k % 2, :], ALU.add).then_inc(full_ready, 1)

            def x1_low(h, k):
                half = slice(h * HALF, (h + 1) * HALF)
                dve.wait_ge(hi_ready, (5 + h) * KT + k + 1)
                nc.vector.tensor_tensor(x1_lo[:, k, half], wout[:, k, half], x1_hi[:, k, half].bitcast(F32),
                                        ALU.subtract).then_inc(lo_ready, 1)

            def some_x1(h, m):
                for k in x1_beside(m):
                    x1_full(h, k)
                for k in x1_beside(m):
                    x1_low(h, k)

            def gate_tile(a2, j, m, h):
                half = slice(h * HALF, (h + 1) * HALF)
                dve.wait_ge(ps_free[j], a2 + 5)
                dve.wait_ge(ple_loaded[j], (a2 - (I0 // 2 - 1)) * 16)
                dve.wait_ge(out_ready, m + (h * KT + 1))
                stt(square[:], tanh_h[:], 1.0, ring_h[:, 1, j, :], ALU.add, ALU.mult).then_inc(tanh_used, 1)
                dve.wait_ge(tanh_used, m + (h * KT + 2))
                stt(result[:, m, half], square[:], 0.5, wout[:, m, half], ALU.mult, ALU.add).then_inc(out_ready, 1)

            with dve.Fori(0, KT // 2) as i:
                for j in range(2):
                    add_square(i + H0 // 2, j, i * 2 + j, 0)
            for m in range(KT):
                if m == 0:
                    variance(3, slice(0, NB // 2))
                    diagonal(3, slice(0, NB // 2))
                some_x1(0, m)
                add_square((H0 + KT + m) // 2, m % 2, m, 1)
            dve.wait_ge(sq_used, 3 * KT)
            dve.sem_inc(tanh_used, 1)
            dve.sem_inc(out_ready, 1)
            for m in range(KT):
                if m == 0:
                    variance(4, slice(NB // 2, NB))
                    diagonal(4, slice(NB // 2, NB))
                some_x1(1, m)
                gate_tile((I0 + m) // 2, m % 2, m, 0)
            with dve.Fori(0, KT // 2) as i:
                for j in range(2):
                    gate_tile(i + (I0 + KT) // 2, j, i * 2 + j, 1)


SHAPES = {"xT": [P, KT, S], "pT": [P, PLE_KT, S], "weights": [P, PLE_STEPS + WTILES, KT * P], "cols": [P, NCOL],
          "masks": [P, 3, P], "positions": [P, S], "sinks_b": [P, HEADS]}


def kernel(x, p, positions, w_in, ln_pre, ln_post, w_dw, b_dw, conv_ln_g, conv_ln_b,
           w_pw, sinks, w_br_conv, w_br_attn, w_out, w_ple_gate, w_ple_proj):
    import numpy as np
    import concourse.bacc as bacc
    from concourse.bass_utils import run_bass_kernel_spmd

    def k_major(w):
        k, n = w.shape
        return w.reshape(k // P, P, n // P, P).transpose(1, 2, 0, 3).reshape(P, n // P, (k // P) * P)

    w_in = k_major(np.asarray(w_in)[0])
    val, glu, cgate, q, k, v, agate, gconv, gattn = np.split(w_in, np.cumsum([8, 8, 8, 8, 1, 1, 8, 8]), axis=1)
    first = np.stack([glu, val, gconv, gattn], axis=2).reshape(P, 4 * KT, KT * P)
    ple = k_major(np.asarray(w_ple_proj)[0]).reshape(P, PLE_STEPS, KT * P)
    weights = np.concatenate([ple, first, k, v, q, cgate, agate] +
                             [k_major(np.asarray(w)[0]) for w in (w_br_attn, w_pw, w_br_conv, w_out, w_ple_gate)], axis=1)
    per_tile = lambda a: np.asarray(a)[0].reshape(KT, P).T
    taps = np.asarray(w_dw)[0].reshape(TAPS, KT, P).transpose(2, 1, 0).reshape(P, KT * TAPS)
    dim = np.arange(P) % HD
    inv = np.where(dim < 16, (500000.0 ** (-(dim % 8) / 8.0)), 0.0).astype(np.float32)
    sgn = np.where(dim < 8, -1.0, 1.0).astype(np.float32)
    cols = np.concatenate([per_tile(a) for a in (ln_pre, ln_post, conv_ln_g, conv_ln_b, b_dw)] +
                          [taps, inv[:, None], sgn[:, None]], axis=1)
    part, free = np.arange(P)[:, None], np.arange(P)[None, :]
    masks = np.stack([part == free, part > free, free > part], axis=1).astype(np.float32)
    order = [2 * (4 * g + j) + par for g in range(2) for par in range(2) for j in range(4)]
    arrays = {
        "xT": np.asarray(x)[0].T.reshape(KT, P, S).transpose(1, 0, 2),
        "pT": np.asarray(p)[0, 0].T.reshape(PLE_KT, P, S).transpose(1, 0, 2),
        "weights": weights, "cols": cols, "masks": masks,
        "positions": np.broadcast_to(np.asarray(positions), (P, S)),
        "sinks_b": np.broadcast_to(np.asarray(sinks)[0][order], (P, HEADS)),
    }
    arrays = {n: np.ascontiguousarray(a) for n, a in arrays.items()}
    nc = bacc.Bacc("TRN2", target_bir_lowering=False, num_devices=1)
    dram = {n: nc.dram_tensor(n, SHAPES[n], mybir.dt.from_np(a.dtype), kind="ExternalInput").ap() for n, a in arrays.items()}
    dram["gates"] = nc.dram_tensor("gates", [P, 3 * KT, S], F32, kind="Internal").ap()
    dram["ple"] = nc.dram_tensor("ple", [P, KT, S], F32, kind="Internal").ap()
    dram["outT"] = nc.dram_tensor("outT", [P, KT, S], F32, kind="ExternalOutput").ap()
    build(nc, dram)
    r = run_bass_kernel_spmd(nc, [arrays], core_ids=[0])
    out = r.results[0]["outT"]
    return out.transpose(1, 0, 2).reshape(D, S).T[None]
```
